# Optimizing a Trainium2 kernel written in Bass

```python
import math
import jax, jax.numpy as jnp
from jax import lax
import numpy as np

D_MODEL = 2048
BATCH = 1
SEQ = 512
DEPTH = 1

CONV_CH = D_MODEL // 2
ATTN_WIDTH = D_MODEL - CONV_CH
HEAD_DIM = 128
N_HEADS = ATTN_WIDTH // HEAD_DIM
CONV_GROUPS = CONV_CH // HEAD_DIM
CONV_WIDTH = 31
DILATED_PATTERNS = ((128, 1), (512, 4), (2048, 16))
FFN_DIM = 5632
FFN_CONV_WIDTH = 3
IN_COLS = 2 * CONV_CH + 3 * ATTN_WIDTH
RMS_EPS = 1e-6
LN_EPS = 1e-5
NEG_BIG = -1e30

kernel_name = "hybrid_conformer_dilated_attn_encoder"

def rmsnorm(x, g):
    xf = x.astype(jnp.float32)
    y = xf * lax.rsqrt(jnp.mean(xf * xf, axis=-1, keepdims=True) + RMS_EPS)
    return (y * g.astype(jnp.float32)).astype(x.dtype)

def layernorm(x, g, b):
    xf = x.astype(jnp.float32)
    mu = jnp.mean(xf, axis=-1, keepdims=True)
    xc = xf - mu
    var = jnp.mean(xc * xc, axis=-1, keepdims=True)
    y = xc * lax.rsqrt(var + LN_EPS)
    return (y * g.astype(jnp.float32) + b.astype(jnp.float32)).astype(x.dtype)

def depthwise_conv_seq(x, w, b):
    k = w.shape[0]
    c = x.shape[-1]
    half = (k - 1) // 2
    y = lax.conv_general_dilated(
        x, w[:, None, :].astype(x.dtype), window_strides=(1,),
        padding=[(half, k - 1 - half)],
        dimension_numbers=("NWC", "WIO", "NWC"),
        feature_group_count=c)
    return y + b.astype(x.dtype)

def alibi_slopes(n_heads):
    return jnp.asarray([2.0 ** (-8.0 * (i + 1) / n_heads) for i in range(n_heads)], jnp.float32)

def dilated_branch(q, k, v, slopes, window, dilation):
    bsz, nh, s_len, hd = q.shape
    r = window // (2 * dilation)
    sub_len = s_len // dilation
    nb = -(-sub_len // r)
    lp = nb * r

    def to_sub(t):
        return t.reshape(bsz, nh, sub_len, dilation, hd).transpose(0, 1, 3, 2, 4)

    qs = jnp.pad(to_sub(q), ((0, 0), (0, 0), (0, 0), (0, lp - sub_len), (0, 0)))
    qs = qs.reshape(bsz, nh, dilation, nb, r, hd)
    pad_kv = ((0, 0), (0, 0), (0, 0), (r, lp - sub_len + r), (0, 0))

    def kv_blocks(t):
        tp = jnp.pad(to_sub(t), pad_kv).reshape(bsz, nh, dilation, nb + 2, r, hd)
        return jnp.concatenate(
            [tp[:, :, :, 0:nb], tp[:, :, :, 1:nb + 1], tp[:, :, :, 2:nb + 2]], axis=4)

    kb = kv_blocks(k)
    vb = kv_blocks(v)

    p_idx = np.arange(r)[:, None]
    c_idx = np.arange(3 * r)[None, :]
    off = c_idx - r - p_idx
    a_k = np.arange(nb)[:, None, None] * r + c_idx[None] - r
    valid = (np.abs(off)[None] <= r) & (a_k >= 0) & (a_k < sub_len)
    dist = jnp.asarray(np.abs(off) * dilation, jnp.float32)

    s = jnp.einsum("bhrnqd,bhrnkd->bhrnqk", qs, kb)
    s = s - slopes[None, :, None, None, None, None] * dist
    s = jnp.where(jnp.asarray(valid), s, NEG_BIG)
    m = jnp.max(s, axis=-1, keepdims=True)
    pexp = jnp.exp(s - m)
    den = jnp.sum(pexp, axis=-1, keepdims=True)
    o = jnp.einsum("bhrnqk,bhrnkd->bhrnqd", pexp, vb) / den
    lse = (m + jnp.log(den))[..., 0]

    o = o.reshape(bsz, nh, dilation, lp, hd)[:, :, :, :sub_len]
    o = o.transpose(0, 1, 3, 2, 4).reshape(bsz, nh, s_len, hd)
    lse = lse.reshape(bsz, nh, dilation, lp)[:, :, :, :sub_len]
    lse = lse.transpose(0, 1, 3, 2).reshape(bsz, nh, s_len)
    return o, lse

def conformer_conv_group(u_a, conv_dw_w, conv_dw_b, conv_ln_g, conv_ln_b):
    val = u_a[..., :CONV_CH]
    gate = u_a[..., CONV_CH:]
    a = val * jax.nn.sigmoid(gate)
    a = depthwise_conv_seq(a, conv_dw_w, conv_dw_b)
    a = layernorm(a, conv_ln_g, conv_ln_b)
    return jax.nn.silu(a)

def dilated_attention_group(u_b, q_norm_g, k_norm_g):
    bsz, s_len, _ = u_b.shape
    q = u_b[..., :ATTN_WIDTH].reshape(bsz, s_len, N_HEADS, HEAD_DIM)
    k = u_b[..., ATTN_WIDTH:2 * ATTN_WIDTH].reshape(bsz, s_len, N_HEADS, HEAD_DIM)
    v = u_b[..., 2 * ATTN_WIDTH:].reshape(bsz, s_len, N_HEADS, HEAD_DIM)
    q = rmsnorm(q, q_norm_g).astype(jnp.float32) * (HEAD_DIM ** -0.5)
    k = rmsnorm(k, k_norm_g).astype(jnp.float32)
    v = v.astype(jnp.float32)
    q, k, v = (t.transpose(0, 2, 1, 3) for t in (q, k, v))
    slopes = alibi_slopes(N_HEADS)
    outs = []
    lses = []
    for window, dilation in DILATED_PATTERNS:
        o, lse = dilated_branch(q, k, v, slopes, window, dilation)
        outs.append(o)
        lses.append(lse)
    wts = jax.nn.softmax(jnp.stack(lses, axis=0), axis=0)
    o = jnp.sum(wts[..., None] * jnp.stack(outs, axis=0), axis=0)
    return o.transpose(0, 2, 1, 3).reshape(bsz, s_len, ATTN_WIDTH)

def conv_ffn(h, w_up, ffn_dw_w, ffn_dw_b, w_down):
    u = h @ w_up
    u = depthwise_conv_seq(u, ffn_dw_w, ffn_dw_b)
    g = u[..., :FFN_DIM]
    val = u[..., FFN_DIM:]
    return (jax.nn.silu(g) * val) @ w_down

def setup_inputs(seed: int = 0) -> dict:
    key = jax.random.key(seed)
    ks = jax.random.split(key, 16)
    f32 = jnp.float32
    nrm = lambda k, shape, scale: jax.random.normal(k, shape, f32) * scale
    return {
        "x": nrm(ks[0], (BATCH, SEQ, D_MODEL), 1.0),
        "norm1_g": 1.0 + nrm(ks[1], (D_MODEL,), 0.02),
        "w_in": nrm(ks[2], (D_MODEL, IN_COLS), D_MODEL ** -0.5),
        "conv_dw_w": nrm(ks[3], (CONV_WIDTH, CONV_CH), CONV_WIDTH ** -0.5),
        "conv_dw_b": nrm(ks[4], (CONV_CH,), 0.01),
        "conv_ln_g": 1.0 + nrm(ks[5], (CONV_CH,), 0.02),
        "conv_ln_b": nrm(ks[6], (CONV_CH,), 0.01),
        "q_norm_g": 1.0 + nrm(ks[7], (HEAD_DIM,), 0.02),
        "k_norm_g": 1.0 + nrm(ks[8], (HEAD_DIM,), 0.02),
        "w_out": nrm(ks[9], (D_MODEL, D_MODEL), D_MODEL ** -0.5),
        "norm2_g": 1.0 + nrm(ks[10], (D_MODEL,), 0.02),
        "w_up": nrm(ks[11], (D_MODEL, 2 * FFN_DIM), D_MODEL ** -0.5),
        "ffn_dw_w": nrm(ks[12], (FFN_CONV_WIDTH, 2 * FFN_DIM), FFN_CONV_WIDTH ** -0.5),
        "ffn_dw_b": nrm(ks[13], (2 * FFN_DIM,), 0.01),
        "w_down": nrm(ks[14], (FFN_DIM, D_MODEL), FFN_DIM ** -0.5),
    }

def reference(x, norm1_g, w_in, conv_dw_w, conv_dw_b, conv_ln_g, conv_ln_b,
              q_norm_g, k_norm_g, w_out, norm2_g, w_up, ffn_dw_w, ffn_dw_b, w_down):
    for _ in range(DEPTH):
        h = rmsnorm(x, norm1_g)
        u = h @ w_in
        a_out = conformer_conv_group(u[..., :2 * CONV_CH], conv_dw_w, conv_dw_b,
                                     conv_ln_g, conv_ln_b)
        b_out = dilated_attention_group(u[..., 2 * CONV_CH:], q_norm_g, k_norm_g)
        mixed = jnp.concatenate([a_out, b_out.astype(x.dtype)], axis=-1)
        x = x + mixed @ w_out
        h2 = rmsnorm(x, norm2_g)
        x = x + conv_ffn(h2, w_up, ffn_dw_w, ffn_dw_b, w_down)
    return x


_drawn_inputs = setup_inputs


def setup_inputs(seed=0):
    import zlib

    import numpy as np

    out = dict(_drawn_inputs(seed))
    spreads = {}
    factors = {'norm1_g': 4.828,
     'conv_dw_b': 21.359,
     'conv_ln_g': 16.969,
     'conv_ln_b': 33.968,
     'q_norm_g': 8.0,
     'k_norm_g': 8.0,
     'norm2_g': 4.09,
     'ffn_dw_b': 8.0}
    for name, (base, spread) in spreads.items():
        noise = np.random.default_rng([zlib.crc32(name.encode()), seed]).standard_normal(out[name].shape)
        drawn = base * np.exp(spread * noise) if base else spread * noise
        out[name] = __import__('jax').numpy.asarray(drawn.astype(out[name].dtype))
    for name, factor in factors.items():
        out[name] = (out[name] * factor).astype(out[name].dtype)
    return out
```

```python
from contextlib import ExitStack

import numpy as np

import concourse.bass as bass
from concourse import mybir

ALU = mybir.AluOpType
ACT = mybir.ActivationFunctionType
F32 = mybir.dt.float32
F32R = mybir.dt.float32r
AX_X = mybir.AxisListType.X

P = 128
S = 512
QT = S // P
D = 2048
DT = D // P
CT = DT // 2
HEADS = 8
TAPS = 31
PAD = TAPS // 2
F = 5632
FT = F // P
KC = 4
NC = 2 * P
PAIRS = CT // 2
GROUPS = FT // KC
PATTERNS = ((128, 1), (512, 4), (2048, 16))

I_SLOTS = 20
A0 = I_SLOTS * PAIRS
B0 = A0 + D // NC
F0 = B0 + 3 * (D // NC)
F1 = F0 + 16
F_SLOTS = 24
LAST = F1 + F_SLOTS * (GROUPS - 1)
SLOTS = LAST + 8

GA, GB, GF = 5 * PAIRS, 5 * PAIRS + 8, 5 * PAIRS + 16

C_G1 = 0
C_G2 = C_G1 + DT
C_CW = C_G2 + DT
C_CB = C_CW + CT * TAPS
C_LG = C_CB + CT
C_LB = C_LG + CT
C_QG = C_LB + CT
C_KG = C_QG + 1
C_FW = C_KG + 1
C_FB = C_FW + 2 * FT * 3
C_ALL = C_FB + 2 * FT

BIAS_W = 2 * S - P
K_ID = 0
K_DIST = K_ID + P
K_LOGN = K_DIST + BIAS_W
K_MEAN_D = K_LOGN + BIAS_W
K_MEAN_C = K_MEAN_D + 1
K_MEAN_H = K_MEAN_C + 1
K_EPS_R = K_MEAN_H + 1
K_EPS_L = K_EPS_R + 1
K_SLOPE = K_EPS_L + 1
K_ALL = K_SLOPE + HEADS

T_FIRST = ["XCOL", "XROW", "Q", "K"]
T_PAIR = ["V0", "V1"] + [f"P{u}" for u in range(8)] + ["Q", "K"]
T_LAST = ["V0", "V1", "MU", "P0", "P1", "VAR", "P2", "ROW"] + [f"P{u}" for u in range(3, 8)]
T_FFN = ["COL", "ROW"]


def t_use(i, name):
    if isinstance(i, str):
        before = len(T_FIRST) + 3 * len(T_PAIR) + (len(T_LAST) if i == "F" else 0)
        return before + (T_LAST if i == "A" else T_FFN).index(name) + 1
    if isinstance(i, int) and i == 0:
        return T_FIRST.index(name) + 1
    return len(T_PAIR) * i + (len(T_FIRST) - len(T_PAIR) + T_PAIR.index(name) + 1)


def taps_of(slot):
    count = {9: 4, 10: 6, 11: 6, 12: 3, 13: 6, 14: 6, 15: 6, 16: 3, 17: 5, 18: 5, 19: 2}
    late = {0: 3, 1: 3, 2: 2, 3: 2}
    at = 0
    for s in sorted(count):
        if s == slot:
            return range(at, at + count[s])
        at += count[s]
    for s in sorted(late):
        if s == slot:
            return range(at, at + late[s])
        at += late[s]
    assert at == 2 * TAPS
    return range(0)


def hybrid_encoder_layer(nc, x_t, w_in, w_out, w_up, w_down, params, consts, out):
    with ExitStack() as ctx:
        def sem(name):
            return ctx.enter_context(nc.semaphore(name))

        start = -(-nc.sbuf_base // 32) * 32

        def place(name, shape, dt, offset):
            size = 4 * int(np.prod(shape[1:]))
            assert offset % 32 == 0 and start + offset + size <= nc.sbuf_usable_end, name
            return nc.alloc_sbuf_tensor_at(name, shape, dt, offset=start + offset), -(-(offset + size) // 32) * 32

        par, o = place("channel_params", [P, C_ALL], F32, 0)
        con, o = place("constants", [P, K_ALL], F32, o)
        qk_gain, o = place("qk_gain", [P, 1], F32, o)
        std_col, o = place("std_col", [P, 8], F32, o)
        rms_col, o = place("rms_col", [P, 4], F32, o)
        rq_col, o = place("rq_col", [P, 8], F32, o)
        rk_col, o = place("rk_col", [P, 8], F32, o)
        neg_max, o = place("neg_max", [P, 2], F32, o)
        row_sum, o = place("row_sum", [P, 2], F32, o)
        row_inv, o = place("row_inv", [P, 2], F32, o)
        rms_row, o = place("rms_row", [P, S], F32, o)
        w_raw, o = place("w_raw", [P, 4, KC * NC], F32, o)
        w_high, o = place("w_high", [P, 2, KC * NC], F32R, o)
        w_low, o = place("w_low", [P, 2, KC * NC], F32R, o)
        squares, o = place("squares", [P, 2, S], F32, o)
        square_sum, o = place("square_sum", [P, 2, S], F32, o)
        res, o = place("residual", [P, DT, S], F32, o)
        r1 = o
        h_high, o = place("h_high", [P, DT, S], F32R, r1)
        h_low, o = place("h_low", [P, DT, S], F32R, o)
        centred_sq, _ = place("centred_sq", [P, CT, S], F32, r1)
        hid_high, f = place("hid_high", [P, KC, S], F32R, r1)
        hid_low, f = place("hid_low", [P, KC, S], F32R, f)
        gated, f = place("gated", [P, KC, S], F32, f)
        up_pad, f = place("up_pad", [P, 2, S + 2], F32, f)
        up_conv, f = place("up_conv", [P, 2, S], F32, f)
        assert f <= o
        r2 = o
        mixed, o = place("mixed", [P, DT, S], F32, r2)
        q_t, o = place("q_t", [P, 2, S], F32, o)
        k_t, o = place("k_t", [P, 2, S], F32, o)
        v_n, o = place("v_n", [P, 2, S], F32, o)
        probs, o = place("probs", [P, 2, S], F32, o)
        probs_t, o = place("probs_t", [P, 2, S], F32, o)
        bias, o = place("bias", [P, BIAS_W], F32, o)
        glu, o = place("glu", [P, 2, S + 2 * PAD], F32, o)
        conv_sum, o = place("conv_sum", [P, S], F32, o)
        ln_mean, o = place("ln_mean", [P, S], F32, o)
        ln_rstd, o = place("ln_rstd", [P, S], F32, o)
        h2_high, g = place("h2_high", [P, DT, S], F32R, r2)
        h2_low, g = place("h2_low", [P, DT, S], F32R, g)

        acc = ctx.enter_context(nc.psum_tensor("acc", [P, 4, S], F32))
        score = ctx.enter_context(nc.psum_tensor("score", [P, 2, S], F32))
        turn = ctx.enter_context(nc.psum_tensor("turn", [P, S], F32))
        attn_o = ctx.enter_context(nc.psum_tensor("attn_o", [P, S], F32))

        ident = con[:, K_ID:K_ID + P]

        def const_col(c):
            return con[:, c:c + 1]

        def param(c):
            return par[:, bass.ds(c, 1)]

        params_in, const_in = sem("params_in"), sem("const_in")
        x_in = [sem(f"x_in{k}") for k in range(4)]
        w_arrived = [sem(f"w_arrived{k}") for k in range(4)]
        w_high_ready, w_low_ready, chunk_done = sem("w_high_ready"), sem("w_low_ready"), sem("chunk_done")
        x_high_ready, x_low_ready = sem("x_high_ready"), sem("x_low_ready")
        squares_ready, squares_added = sem("squares_ready"), sem("squares_added")
        emptied = sem("emptied")
        turn_made, turn_read = sem("turn_made"), sem("turn_read")
        inverse_ready, gain_ready, pads_ready, sum_cleared = (sem(n) for n in (
            "inverse_ready", "gain_ready", "pads_ready", "sum_cleared"))
        sigmoid_ready, glu_ready, tap_done, conv_added = (sem(n) for n in (
            "sigmoid_ready", "glu_ready", "tap_done", "conv_added"))
        head_squares, k_spread, k_ready = sem("head_squares"), sem("k_spread"), sem("k_ready")
        bias_ready, score_made, score_read, max_ready, exp_done, sum_inverted, probs_ready, pv_done, o_read = (
            sem(n) for n in ("bias_ready", "score_made", "score_read", "max_ready", "exp_done",
                             "sum_inverted", "probs_ready", "pv_done", "o_read"))
        centred, centred_squares, scaled, conv_out = (sem(n) for n in (
            "centred", "centred_squares", "scaled", "conv_out"))
        mix_high_ready, mix_low_ready = sem("mix_high_ready"), sem("mix_low_ready")
        h2_high_ready, h2_low_ready, res_squares, res_squares_added = (sem(n) for n in (
            "h2_high_ready", "h2_low_ready", "res_squares", "res_squares_added"))
        ffn_pads, up_mid, up_side, gate_act, hidden_ready, hid_high_ready, hid_low_ready = (sem(n) for n in (
            "ffn_pads", "up_mid", "up_side", "gate_act", "hidden_ready", "hid_high_ready", "hid_low_ready"))
        out_written = sem("out_written")

        def weight_slab(w, tile0, col):
            rows = w.rearrange("(t p) n -> p t n", p=P)
            return rows[:, bass.ds(tile0, KC), bass.ds(col, NC)]

        def in_slab(i, s):
            return weight_slab(w_in, KC * (s % 4), 4 * NC * (s // 4) + NC * i)

        def ffn_slab(g, s):
            if s < 8:
                return weight_slab(w_up, KC * (s % 4), KC * P * g + NC * (s // 4))
            if s < 16:
                return weight_slab(w_down, KC * (g - 1), NC * (s - 8))
            return weight_slab(w_up, KC * (s % 4), KC * P * g + (F + NC * ((s - 16) // 4)))

        B_TILES = (0, KC, 3 * KC)
        FIRST_SLOTS = [*range(8), *range(16, F_SLOTS)]

        def up_group(g, y):
            if isinstance(g, int) and g == 0:
                return GF + y
            return 12 * g + (GF - 8 + (y if y < 2 else y + 8))

        def down_group(g, n):
            if isinstance(g, int) and g == GROUPS - 1:
                return GF + 4 + 12 * (GROUPS - 1) + n
            return 12 * g + (GF + 6 + n)

        block = ctx.enter_context(nc.Block())

        @block.sync
        def _(sp):
            def fetch(c, s, slab, wait=True):
                if wait:
                    sp.wait_ge(w_low_ready, c - 3)
                sp.dma_start(w_raw[:, s % 4, :].rearrange("p (t n) -> p t n", n=NC), slab).then_inc(
                    w_arrived[s % 4], 16)

            sp.dma_start(par[:], params).then_inc(params_in, 16)
            for k in range(4):
                sp.dma_start(res[:, KC * k:KC * (k + 1), :], x_t[:, KC * k:KC * (k + 1), :]).then_inc(x_in[k], 16)
                fetch(k, k, in_slab(0, k), wait=False)
            sp.dma_start(con[:], consts).then_inc(const_in, 16)
            for s in range(4, I_SLOTS):
                fetch(s, s, in_slab(0, s))
            with sp.Fori(1, PAIRS) as i:
                for s in range(I_SLOTS):
                    fetch(I_SLOTS * i + s, s, in_slab(i, s))
            for n in range(8):
                fetch(A0 + n, A0 + n, weight_slab(w_out, 2 * KC, NC * n))
            for n in range(8):
                for b in range(3):
                    fetch(B0 + 3 * n + b, 3 * n + b, weight_slab(w_out, B_TILES[b], NC * n))
            for l, s in enumerate(FIRST_SLOTS):
                fetch(F0 + l, l, ffn_slab(0, s))
            with sp.Fori(1, GROUPS) as g:
                for s in range(F_SLOTS):
                    fetch(F_SLOTS * g + (F1 - F_SLOTS + s), s, ffn_slab(g, s))
            for s in range(8):
                fetch(LAST + s, s, ffn_slab(GROUPS, 8 + s))
            for n in range(8):
                sp.wait_ge(emptied, down_group(GROUPS - 1, n) + 1)
                sp.dma_start(out[:, 2 * n:2 * n + 2, :], res[:, 2 * n:2 * n + 2, :]).then_inc(out_written, 16)
            sp.wait_ge(out_written, 16 * 8)

        @block.gpsimd
        def _(pool):
            nc.gpsimd.memset(conv_sum[:], 0.0).then_inc(sum_cleared, 1)

            def add_tile(i, t):
                first = isinstance(i, int) and t == 0
                if first:
                    pool.wait_ge(sum_cleared, 1)
                else:
                    pool.wait_ge(conv_added, 2 * i + t)
                if t == 0:
                    pool.wait_ge(tap_done, 2 * TAPS * i + 2 * TAPS)
                nc.gpsimd.tensor_tensor(conv_sum[:].rearrange("p (o n) -> p o n", o=1),
                                        conv_sum[:].rearrange("p (o n) -> p o n", o=1),
                                        mixed[:, bass.ds(2 * i + t, 1), :], ALU.add).then_inc(conv_added, 1)

            add_tile(0, 0)
            add_tile(0, 1)
            with pool.Fori(1, PAIRS) as i:
                add_tile(i, 0)
                add_tile(i, 1)

        @block.scalar
        def _(act):
            def split_high(c, s, buffer_used=True):
                act.wait_ge(w_arrived[s % 4], 4 * (c - s % 4) + 16)
                if buffer_used:
                    act.wait_ge(chunk_done, c - 1)
                nc.scalar.activation(w_high[:, s % 2, :], w_raw[:, s % 4, :], ACT.Copy).then_inc(w_high_ready, 1)

            def x_chunk(k):
                act.wait_ge(x_in[k], 16)
                for j in range(KC * k, KC * (k + 1)):
                    nc.scalar.activation(h_high[:, j, :], res[:, j, :], ACT.Copy, scale=param(C_G1 + j)
                                         ).then_inc(x_high_ready, 1)
                for n in range(2 * k, 2 * k + 2):
                    if n:
                        act.wait_ge(squares_added, n)
                    nc.scalar.activation(squares[:], res[:, 2 * n:2 * n + 2, :], ACT.Square).then_inc(squares_ready, 1)

            def turn_copy(i, name, dst):
                act.wait_ge(turn_made, t_use(i, name))
                nc.scalar.activation(dst, turn[:], ACT.Copy).then_inc(turn_read, 1)

            def turn_sqrt(i, name, width, eps):
                act.wait_ge(turn_made, t_use(i, name))
                nc.scalar.activation(std_col[:, 0:width], turn[:, 0:width], ACT.Sqrt, bias=const_col(eps)
                                     ).then_inc(turn_read, 1)

            def exp_unit(j, u):
                act.wait_ge(max_ready, 8 * j + (u + 1))
                nc.scalar.activation(probs[:, u % 2, :], probs[:, u % 2, :], ACT.Exp, bias=neg_max[:, u % 2:u % 2 + 1],
                                     accum_out=row_sum[:, u % 2:u % 2 + 1]).then_inc(exp_done, 1)

            def normalise_unit(j, u):
                act.wait_ge(sum_inverted, 8 * j + (u + 1))
                nc.scalar.activation(probs[:, u % 2, :], probs[:, u % 2, :], ACT.Copy,
                                     scale=row_inv[:, u % 2:u % 2 + 1]).then_inc(probs_ready, 1)

            def attention_slot(i, j, s):
                if s in (1, 2):
                    turn_copy(i, f"V{s - 1}", v_n[:, s - 1, :])
                if 3 <= s <= 10:
                    u = s - 3
                    if u >= 2:
                        act.wait_ge(pv_done, 8 * j + (u - 1))
                    turn_copy(i, f"P{u}", probs_t[:, u % 2, :])
                if 2 <= s <= 9:
                    normalise_unit(j, s - 2)
                if 1 <= s <= 8:
                    exp_unit(j, s - 1)
                if s in (7, 11):
                    hh = s // 11
                    act.wait_ge(pv_done, 8 * j + (4 * hh + 4))
                    nc.scalar.activation(mixed[:, bass.ds(2 * j + (CT + hh), 1), :], attn_o[:].rearrange(
                        "p (o n) -> p o n", o=1), ACT.Copy).then_inc(o_read, 1)

            def iteration(i):
                first = isinstance(i, int)
                c0 = I_SLOTS * i
                for s in range(I_SLOTS):
                    split_high(c0 + (s + 1), s + 1, buffer_used=not (first and s == 0))
                    if first and s < 3:
                        x_chunk(s + 1)
                    if first and s == 5:
                        turn_sqrt(0, "XCOL", 4, K_EPS_R)
                    if first and s == 6:
                        turn_copy(0, "XROW", rms_row[:])
                    if not first:
                        attention_slot(i, i - 1, s)
                    if s == 8:
                        act.wait_ge(emptied, 5 * i + 2)
                        nc.scalar.activation(q_t[:], q_t[:], ACT.Sigmoid).then_inc(sigmoid_ready, 1)
                    if s == 12:
                        act.wait_ge(emptied, 5 * i + 3)
                        nc.scalar.activation(squares[:], q_t[:], ACT.Square).then_inc(head_squares, 1)
                    if s == 14:
                        turn_sqrt(i, "Q", 8, K_EPS_R)
                    if s == 16:
                        act.wait_ge(emptied, 5 * i + 4)
                        act.wait_ge(turn_made, t_use(i, "Q"))
                        nc.scalar.activation(squares[:], k_t[:], ACT.Square).then_inc(head_squares, 1)
                    if s == 17:
                        act.wait_ge(inverse_ready, 2 * i + 2)
                        turn_sqrt(i, "K", 8, K_EPS_R)

            def mix_high(pair):
                nc.scalar.activation(h_high[:, 2 * pair:2 * pair + 2, :], mixed[:, 2 * pair:2 * pair + 2, :],
                                     ACT.Copy).then_inc(mix_high_ready, 1)

            act.wait_ge(params_in, 16)
            x_chunk(0)
            split_high(0, 0, buffer_used=False)
            iteration(0)
            with act.Fori(1, PAIRS) as i:
                iteration(i)

            act.wait_ge(chunk_done, A0)
            act.wait_ge(o_read, 4)
            mix_high(4)
            mix_high(5)
            for s in range(8):
                split_high(A0 + s + 1, s + 1)
                attention_slot("A", 3, s)
                if s == 2:
                    turn_copy("A", "MU", ln_mean[:])
                if s == 4:
                    for n in range(4):
                        act.wait_ge(centred, n + 1)
                        nc.scalar.activation(centred_sq[:, 2 * n:2 * n + 2, :], mixed[:, 2 * n:2 * n + 2, :],
                                             ACT.Square).then_inc(centred_squares, 1)
                    turn_sqrt("A", "VAR", 4, K_EPS_L)
                if s == 5:
                    turn_copy("A", "ROW", ln_rstd[:])
                if s == 7:
                    for n in range(4):
                        act.wait_ge(scaled, n + 1)
                        for j in (2 * n, 2 * n + 1):
                            nc.scalar.activation(mixed[:, j, :], mixed[:, j, :], ACT.Silu, scale=param(C_LG + j),
                                                 bias=param(C_LB + j)).then_inc(conv_out, 1)
                        act.wait_ge(conv_out, 2 * n + 2)
                        mix_high(n)

            def h2_high_pair(n):
                act.wait_ge(emptied, GB + n + 1)
                for j in (2 * n, 2 * n + 1):
                    nc.scalar.activation(h2_high[:, j, :], res[:, j, :], ACT.Copy, scale=param(C_G2 + j)
                                         ).then_inc(h2_high_ready, 1)
                if n:
                    act.wait_ge(res_squares_added, n)
                nc.scalar.activation(squares[:], res[:, 2 * n:2 * n + 2, :], ACT.Square).then_inc(res_squares, 1)

            for n in range(8):
                for b in range(3):
                    c = B0 + 3 * n + b
                    split_high(c + 1, c + 1)
                    if n == 0 and b == 0:
                        attention_slot("A", 3, 8)
                    if n == 0 and b == 1:
                        for s in (9, 10, 11):
                            attention_slot("A", 3, s)
                        act.wait_ge(o_read, 8)
                        mix_high(6)
                        mix_high(7)
                    if n and b == 0:
                        if n == 1:
                            act.wait_ge(mix_low_ready, 8)
                        h2_high_pair(n - 1)

            def up_act(g, y):
                act.wait_ge(emptied, up_group(g, y) + 1)
                if y == 0 and needs_wait(g):
                    act.wait_ge(hidden_ready, 2 * g)
                if y == 3:
                    act.wait_ge(hidden_ready, 2 * g + 1)
                for t in range(2):
                    f = FT * (y // 2) + 2 * (y % 2) + t
                    nc.scalar.activation(up_conv[:, t, :], up_pad[:, t, 1:S + 1], ACT.Identity,
                                         scale=param(3 * KC * g + (C_FW + 3 * f + 1)),
                                         bias=param(KC * g + (C_FB + f))).then_inc(up_mid, 1)

            def gate_swish(g, y):
                act.wait_ge(up_side, 16 * g + (4 * y + 4))
                if needs_wait(g):
                    act.wait_ge(hid_low_ready, 2 * g + (y - 1))
                nc.scalar.activation(gated[:, 2 * y:2 * y + 2, :], up_conv[:], ACT.Silu).then_inc(gate_act, 1)

            def hidden_high(g, y):
                act.wait_ge(hidden_ready, 2 * g + (y + 1))
                if y == 0 and needs_wait(g):
                    act.wait_ge(chunk_done, F_SLOTS * g + (F1 - F_SLOTS + 16))
                nc.scalar.activation(hid_high[:, 2 * y:2 * y + 2, :], gated[:, 2 * y:2 * y + 2, :], ACT.Copy
                                     ).then_inc(hid_high_ready, 1)

            def ffn_slot(g, s, c):
                first = isinstance(g, int)
                split_high(c + 1, s + 1)
                if s == 0 and not first:
                    up_act(g - 1, 3)
                if s == 2 and not first:
                    hidden_high(g - 1, 1)
                if s == 4:
                    up_act(g, 0)
                if s == 5:
                    gate_swish(g, 0)
                if s == (16 if first else 8):
                    up_act(g, 1)
                if s == (17 if first else 9):
                    gate_swish(g, 1)
                if s == 20:
                    up_act(g, 2)
                if s == 22:
                    hidden_high(g, 0)

            for l, s in enumerate(FIRST_SLOTS):
                ffn_slot(0, s, F0 + l)
                if l == 0:
                    h2_high_pair(7)
                if l == 2:
                    turn_sqrt("F", "COL", 4, K_EPS_R)
                if l == 3:
                    turn_copy("F", "ROW", rms_row[:])
            with act.Fori(1, GROUPS) as g:
                for s in range(F_SLOTS):
                    ffn_slot(g, s, F_SLOTS * g + (F1 - F_SLOTS + s))
            split_high(LAST + 1, 1)
            up_act(GROUPS - 1, 3)
            hidden_high(GROUPS - 1, 1)
            for s in range(2, 8):
                split_high(LAST + s, s)

        @block.vector
        def _(dve):
            v = nc.vector

            def split_low(c, s):
                dve.wait_ge(w_high_ready, c + 1)
                v.tensor_tensor(w_low[:, s % 2, :], w_raw[:, s % 4, :], w_high[:, s % 2, :].bitcast(F32),
                                ALU.subtract).then_inc(w_low_ready, 1)

            def add_squares(n, ready, added):
                dve.wait_ge(ready, n + 1)
                if n == 0:
                    v.tensor_copy(square_sum[:], squares[:]).then_inc(added, 1)
                else:
                    dve.wait_ge(added, n)
                    v.tensor_tensor(square_sum[:], square_sum[:], squares[:], ALU.add).then_inc(added, 1)

            def x_chunk(k):
                for j in range(KC * k, KC * (k + 1)):
                    dve.wait_ge(x_high_ready, j + 1)
                    v.scalar_tensor_tensor(out=h_low[:, j, :], in0=res[:, j, :], scalar=param(C_G1 + j),
                                           in1=h_high[:, j, :].bitcast(F32), op0=ALU.mult, op1=ALU.subtract
                                           ).then_inc(x_low_ready, 1)
                for n in range(2 * k, 2 * k + 2):
                    add_squares(n, squares_ready, squares_added)

            def spread(row):
                return row[:].rearrange("p (o n) -> p o n", o=1).broadcast_to([P, 2, S])

            def scale_out(c_done, src, dst):
                dve.wait_ge(chunk_done, c_done)
                v.tensor_tensor(dst, src, spread(rms_row), ALU.mult).then_inc(emptied, 1)

            def invert(i, name, dst, width):
                dve.wait_ge(turn_read, t_use(i, name))
                v.reciprocal(dst[:, 0:width], std_col[:, 0:width]).then_inc(inverse_ready, 1)

            def taps(i, steps):
                for m in steps:
                    k, t = m // 2, m % 2
                    y = mixed[:, bass.ds(2 * i + t, 1), :]
                    src = glu[:, t:t + 1, k:k + S]
                    w = param(2 * TAPS * i + (C_CW + TAPS * t + k))
                    if k == 0:
                        v.tensor_scalar(y, src, w, param(2 * i + (C_CB + t)), ALU.mult, ALU.add).then_inc(tap_done, 1)
                    else:
                        dve.wait_ge(tap_done, 2 * TAPS * i + (m - 1))
                        v.scalar_tensor_tensor(out=y, in0=src, scalar=w, in1=y, op0=ALU.mult, op1=ALU.add
                                               ).then_inc(tap_done, 1)

            def bias_table(j, hh):
                v.scalar_tensor_tensor(out=bias[:], in0=con[:, K_DIST:K_DIST + BIAS_W],
                                       scalar=con[:, bass.ds(2 * j + (K_SLOPE + hh), 1)],
                                       in1=con[:, K_LOGN:K_LOGN + BIAS_W], op0=ALU.mult, op1=ALU.add
                                       ).then_inc(bias_ready, 1)

            def score_unit(i, j, u):
                dve.wait_ge(score_made, 8 * j + (u + 1))
                dve.wait_ge(bias_ready, 2 * j + (u // 4 + 1))
                if u >= 2:
                    dve.wait_ge(turn_made, t_use(i, f"P{u - 2}"))
                x0 = P * (QT - 1 - u % QT)
                v.scalar_tensor_tensor(out=probs[:, u % 2, :], in0=score[:, u % 2, :], scalar=rq_col[:, u:u + 1],
                                       in1=bias[:, x0:x0 + S], op0=ALU.mult, op1=ALU.add).then_inc(score_read, 1)
                dve.wait_ge(score_read, 8 * j + (u + 1))
                v.tensor_reduce(neg_max[:, u % 2:u % 2 + 1], probs[:, u % 2, :], AX_X, ALU.max, negate=True
                                ).then_inc(max_ready, 1)

            def invert_sum(j, u):
                dve.wait_ge(exp_done, 8 * j + (u + 1))
                v.reciprocal(row_inv[:, u % 2:u % 2 + 1], row_sum[:, u % 2:u % 2 + 1]).then_inc(sum_inverted, 1)

            def attention_slot(i, j, s):
                if 2 <= s <= 9:
                    invert_sum(j, s - 2)
                if s == 0:
                    bias_table(j, 0)
                if s == 5:
                    bias_table(j, 1)
                if 1 <= s <= 8:
                    score_unit(i, j, s - 1)

            def v_out(i):
                scale_out(I_SLOTS * i + I_SLOTS, score[:], mixed[:, DT - 2:DT, :])

            def iteration(i):
                first = isinstance(i, int)
                c0 = I_SLOTS * i
                for s in range(I_SLOTS):
                    if s == 0 and not first:
                        v_out(i - 1)
                    if s == (7 if first else 4):
                        if first:
                            dve.wait_ge(turn_read, t_use(0, "XROW"))
                        scale_out(c0 + 4, acc[:, 0:2, :], mixed[:, bass.ds(2 * i, 2), :])
                    if s == 8:
                        if not first:
                            dve.wait_ge(score_made, 8 * i)
                        scale_out(c0 + 8, acc[:, 2:4, :], q_t[:])
                    if s == 12:
                        scale_out(c0 + 12, acc[:, 0:2, :], q_t[:])
                    if s == 15:
                        invert(i, "Q", rq_col, 8)
                    if s == 16:
                        scale_out(c0 + 16, acc[:, 2:4, :], k_t[:])
                    if s == 18:
                        invert(i, "K", rk_col, 8)
                    split_low(c0 + (s + 1), s + 1)
                    if first and s < 3:
                        x_chunk(s + 1)
                    if first and s == 5:
                        invert(0, "XCOL", rms_col, 4)
                    if not first:
                        attention_slot(i, i - 1, s)
                        if s < 4:
                            taps(i - 1, taps_of(s))
                    if s == 9:
                        dve.wait_ge(sigmoid_ready, i + 1)
                        if first:
                            dve.wait_ge(pads_ready, 2)
                        v.tensor_tensor(glu[:, :, PAD:PAD + S], mixed[:, bass.ds(2 * i, 2), :], q_t[:], ALU.mult
                                        ).then_inc(glu_ready, 1)
                        dve.wait_ge(glu_ready, i + 1)
                    if s >= 9:
                        taps(i, taps_of(s))
                    if s == 19:
                        dve.wait_ge(k_spread, i + 1)
                        for hh, bank in ((0, turn), (1, attn_o)):
                            v.scalar_tensor_tensor(out=k_t[:, hh, :], in0=k_t[:, hh, :], scalar=qk_gain[:, 0:1],
                                                   in1=bank[:], op0=ALU.mult, op1=ALU.mult).then_inc(k_ready, 1)

            def mix_low(n, pair):
                dve.wait_ge(mix_high_ready, n + 1)
                v.tensor_tensor(h_low[:, 2 * pair:2 * pair + 2, :], mixed[:, 2 * pair:2 * pair + 2, :],
                                h_high[:, 2 * pair:2 * pair + 2, :].bitcast(F32), ALU.subtract
                                ).then_inc(mix_low_ready, 1)

            def res_add(n, group, c_done):
                dve.wait_ge(chunk_done, c_done)
                pair = group % 2 if isinstance(group, int) else n % 2
                v.tensor_tensor(res[:, 2 * n:2 * n + 2, :], res[:, 2 * n:2 * n + 2, :],
                                acc[:, 2 * pair:2 * pair + 2, :], ALU.add).then_inc(emptied, 1)

            v.memset(glu[:, :, 0:PAD], 0.0).then_inc(pads_ready, 1)
            v.memset(glu[:, :, PAD + S:], 0.0).then_inc(pads_ready, 1)
            dve.wait_ge(params_in, 16)
            v.scalar_tensor_tensor(out=qk_gain[:], in0=param(C_QG), scalar=float(P) ** -0.5, in1=param(C_KG),
                                   op0=ALU.mult, op1=ALU.mult).then_inc(gain_ready, 1)
            x_chunk(0)
            split_low(0, 0)
            dve.wait_ge(gain_ready, 1)
            iteration(0)
            dve.wait_ge(const_in, 16)
            with dve.Fori(1, PAIRS) as i:
                iteration(i)

            v_out(PAIRS - 1)
            mix_low(0, 4)
            mix_low(1, 5)
            for s in range(8):
                if s:
                    res_add(s - 1, GA + s - 1, A0 + s)
                split_low(A0 + s + 1, s + 1)
                attention_slot("A", 3, s)
                if s == 0:
                    for late in range(4):
                        taps(PAIRS - 1, taps_of(late))
                if s == 3:
                    dve.wait_ge(turn_read, t_use("A", "MU"))
                    for n in range(4):
                        v.tensor_tensor(mixed[:, 2 * n:2 * n + 2, :], mixed[:, 2 * n:2 * n + 2, :], spread(ln_mean),
                                        ALU.subtract).then_inc(centred, 1)
                if s == 4:
                    invert("A", "VAR", rms_col, 4)
                if s == 6:
                    dve.wait_ge(turn_read, t_use("A", "ROW"))
                    dve.wait_ge(centred_squares, 4)
                    for n in range(4):
                        v.tensor_tensor(mixed[:, 2 * n:2 * n + 2, :], mixed[:, 2 * n:2 * n + 2, :], spread(ln_rstd),
                                        ALU.mult).then_inc(scaled, 1)

            def h2_low_pair(n):
                for j in (2 * n, 2 * n + 1):
                    dve.wait_ge(h2_high_ready, j + 1)
                    v.scalar_tensor_tensor(out=h2_low[:, j, :], in0=res[:, j, :], scalar=param(C_G2 + j),
                                           in1=h2_high[:, j, :].bitcast(F32), op0=ALU.mult, op1=ALU.subtract
                                           ).then_inc(h2_low_ready, 1)
                add_squares(n, res_squares, res_squares_added)

            for n in range(8):
                for b in range(3):
                    c = B0 + 3 * n + b
                    if n == 0 and b == 0:
                        res_add(7, GA + 7, A0 + 8)
                        for m in range(4):
                            mix_low(2 + m, m)
                    if n and b == 0:
                        res_add(n - 1, GB + n - 1, c)
                    split_low(c + 1, c + 1)
                    if n == 0 and b == 0:
                        attention_slot("A", 3, 8)
                    if n == 0 and b == 1:
                        attention_slot("A", 3, 9)
                        mix_low(6, 6)
                        mix_low(7, 7)
                    if n and b == 1:
                        h2_low_pair(n - 1)

            def up_out(g, y, c_done):
                if y or needs_wait(g):
                    dve.wait_ge(up_mid, 8 * g + 2 * y)
                pair = y % 2
                scale_out(c_done, acc[:, 2 * pair:2 * pair + 2, :], up_pad[:, :, 1:S + 1])

            def up_taps(g, y):
                for k in (0, 2):
                    for t in range(2):
                        f = FT * (y // 2) + 2 * (y % 2) + t
                        if k == 0:
                            dve.wait_ge(up_mid, 8 * g + (2 * y + t + 1))
                        else:
                            dve.wait_ge(up_side, 16 * g + (4 * y + t + 1))
                        v.scalar_tensor_tensor(out=up_conv[:, t, :], in0=up_pad[:, t, k:k + S],
                                               scalar=param(3 * KC * g + (C_FW + 3 * f + k)), in1=up_conv[:, t, :],
                                               op0=ALU.mult, op1=ALU.add).then_inc(up_side, 1)

            def hidden(g, y):
                dve.wait_ge(up_side, 16 * g + (4 * y + 12))
                dve.wait_ge(gate_act, 2 * g + (y + 1))
                v.tensor_tensor(gated[:, 2 * y:2 * y + 2, :], gated[:, 2 * y:2 * y + 2, :], up_conv[:], ALU.mult
                                ).then_inc(hidden_ready, 1)

            def hidden_low(g, y):
                dve.wait_ge(hid_high_ready, 2 * g + (y + 1))
                v.tensor_tensor(hid_low[:, 2 * y:2 * y + 2, :], gated[:, 2 * y:2 * y + 2, :],
                                hid_high[:, 2 * y:2 * y + 2, :].bitcast(F32), ALU.subtract).then_inc(hid_low_ready, 1)

            def ffn_slot(g, s, c):
                first = isinstance(g, int)
                if s == 0 and not first:
                    up_out(g - 1, 3, c)
                if s == 4:
                    if first:
                        dve.wait_ge(turn_read, t_use("F", "ROW"))
                    up_out(g, 0, c)
                if s == (16 if first else 8):
                    up_out(g, 1, c)
                if 9 <= s <= 16 and not first:
                    res_add(s - 9, g, c)
                if s == 20:
                    up_out(g, 2, c)
                split_low(c + 1, s + 1)
                if s == 0 and not first:
                    up_taps(g - 1, 3)
                if s == 1 and not first:
                    hidden(g - 1, 1)
                if s == 3 and not first:
                    hidden_low(g - 1, 1)
                if s == 4:
                    up_taps(g, 0)
                if s == (16 if first else 8):
                    up_taps(g, 1)
                if s == 20:
                    up_taps(g, 2)
                if s == 21:
                    hidden(g, 0)
                if s == 23:
                    hidden_low(g, 0)

            res_add(7, GB + 7, F0)
            for n in range(2):
                v.memset(up_pad[:, :, n * (S + 1):n * (S + 1) + 1], 0.0).then_inc(ffn_pads, 1)
            dve.wait_ge(ffn_pads, 2)
            for l, s in enumerate(FIRST_SLOTS):
                ffn_slot(0, s, F0 + l)
                if l == 0:
                    h2_low_pair(7)
                if l == 2:
                    invert("F", "COL", rms_col, 4)
            with dve.Fori(1, GROUPS) as g:
                for s in range(F_SLOTS):
                    ffn_slot(g, s, F_SLOTS * g + (F1 - F_SLOTS + s))
            up_out(GROUPS - 1, 3, LAST)
            split_low(LAST + 1, 1)
            up_taps(GROUPS - 1, 3)
            hidden(GROUPS - 1, 1)
            hidden_low(GROUPS - 1, 1)
            for n in range(8):
                if n < 6:
                    split_low(LAST + n + 2, n + 2)
                res_add(n, n, LAST + n + 1)

        @block.tensor
        def _(pe):
            mm = nc.tensor.matmul

            def multiply(c, s, dst, high, low, first, last, ready=None, middle=None):
                pe.wait_ge(w_low_ready, c + 1)
                for j in range(KC):
                    if ready is not None:
                        ready(j)
                    if middle is not None and j == KC // 2:
                        middle()
                    for t in range(2):
                        at = NC * j + P * t
                        wh, wl = w_high[:, s % 2, at:at + P], w_low[:, s % 2, at:at + P]
                        mm(dst[:, t, :], wh, high(j), start=first and j == 0, stop=False)
                        mm(dst[:, t, :], wh, low(j), start=False, stop=False)
                        done = mm(dst[:, t, :], wl, high(j), start=False, stop=last and j == KC - 1)
                done.then_inc(chunk_done, 1)

            def h_tiles(tile0):
                return (lambda j: h_high[:, tile0 + j, :]), (lambda j: h_low[:, tile0 + j, :])

            def next_turn(i, name):
                if not (i == 0 and name == "XCOL" if isinstance(i, int) else False):
                    pe.wait_ge(turn_read, t_use(i, name) - 1)

            def token_sums(tiles, col, n_out):
                for t in range(QT):
                    for n, tile in enumerate(tiles):
                        last = mm(turn[:, t:t + 1], tile[:, P * t:P * (t + 1)], const_col(col), start=n == 0,
                                  stop=n == len(tiles) - 1)
                last.then_inc(turn_made, 1)

            def head_sums():
                for hh in range(2):
                    for t in range(QT):
                        last = mm(turn[:, QT * hh + t:QT * hh + t + 1], squares[:, hh, P * t:P * (t + 1)],
                                  const_col(K_MEAN_H), start=True, stop=True)
                last.then_inc(turn_made, 1)

            def spread_cols(bank, cols):
                for t in range(QT):
                    last = mm(bank[:, P * t:P * (t + 1)], cols[:, t:t + 1].broadcast_to([P, P]), ident,
                              start=True, stop=True)
                return last

            def attention_slot(i, j, s):
                if s == 1:
                    pe.wait_ge(k_ready, 2 * j + 2)
                    pe.wait_ge(emptied, 5 * j + 5)
                if s in (1, 2):
                    next_turn(i, f"V{s - 1}")
                    for t in range(QT):
                        last = nc.tensor.transpose(turn[:, P * t:P * (t + 1)],
                                                   mixed[:, DT - 3 + s, P * t:P * (t + 1)], ident)
                    last.then_inc(turn_made, 1)
                if 4 <= s <= 11:
                    u = s - 4
                    pe.wait_ge(turn_read, t_use(i, f"P{u}"))
                    if u == 4:
                        pe.wait_ge(o_read, 2 * j + 1)
                    hh, q0 = u // 4, P * (u % 4)
                    for t in range(QT):
                        last = mm(attn_o[:, q0:q0 + P], v_n[:, hh, P * t:P * (t + 1)],
                                  probs_t[:, u % 2, P * t:P * (t + 1)], start=t == 0, stop=t == QT - 1)
                    last.then_inc(pv_done, 1)
                if 3 <= s <= 10:
                    u = s - 3
                    next_turn(i, f"P{u}")
                    pe.wait_ge(probs_ready, 8 * j + (u + 1))
                    for t in range(QT):
                        last = nc.tensor.transpose(turn[:, P * t:P * (t + 1)], probs[:, u % 2, P * t:P * (t + 1)], ident)
                    last.then_inc(turn_made, 1)
                if 1 <= s <= 8:
                    u = s - 1
                    if u >= 2:
                        pe.wait_ge(score_read, 8 * j + (u - 1))
                    hh, q0 = u // 4, P * (u % 4)
                    mm(score[:, u % 2, :], q_t[:, hh, q0:q0 + P], k_t[:, hh, :], start=True, stop=True
                       ).then_inc(score_made, 1)

            def iteration(i):
                first = isinstance(i, int)
                c0 = I_SLOTS * i
                for s in range(I_SLOTS):
                    if first and s == 4:
                        pe.wait_ge(const_in, 16)
                    if first and s == 5:
                        pe.wait_ge(squares_added, 8)
                        token_sums([square_sum[:, 0, :], square_sum[:, 1, :]], K_MEAN_D, 4)
                    if first and s == 6:
                        pe.wait_ge(inverse_ready, 1)
                        spread_cols(turn, rms_col).then_inc(turn_made, 1)
                    if not first:
                        attention_slot(i, i - 1, s)
                    if s == 14:
                        next_turn(i, "Q")
                        pe.wait_ge(head_squares, 2 * i + 1)
                        head_sums()
                    if s == 17:
                        next_turn(i, "K")
                        pe.wait_ge(head_squares, 2 * i + 2)
                        head_sums()
                    if s == 19:
                        pe.wait_ge(inverse_ready, 2 * i + 3)
                        if not first:
                            pe.wait_ge(o_read, 2 * i)
                        spread_cols(turn, rk_col[:, 0:QT])
                        spread_cols(attn_o, rk_col[:, QT:2 * QT]).then_inc(k_spread, 1)
                    y = s // 4
                    if s % 4 == 0 and y in (2, 3):
                        pe.wait_ge(emptied, 5 * i + (y - 1))
                    if s % 4 == 0 and y in (0, 1) and not first:
                        pe.wait_ge(emptied, 5 * i + (y - 2))
                    if s % 4 == 0 and y == 4 and not first:
                        pe.wait_ge(score_read, 8 * i)
                    dst = score if y == 4 else acc[:, 2 * (y % 2):2 * (y % 2) + 2, :]
                    tile0 = KC * (s % 4)
                    ready = None
                    if first and s < 4:
                        def ready(j, tile0=tile0):
                            pe.wait_ge(x_low_ready, tile0 + j + 1)
                    multiply(c0 + s, s, dst, *h_tiles(tile0), s % 4 == 0, s % 4 == 3, ready)

            iteration(0)
            with pe.Fori(1, PAIRS) as i:
                iteration(i)

            def layer_norm_mean():
                next_turn("A", "MU")
                pe.wait_ge(conv_added, CT)
                mm(turn[:], const_col(K_MEAN_C).broadcast_to([P, P]), conv_sum[:], start=True, stop=True
                   ).then_inc(turn_made, 1)

            def layer_norm_variance():
                next_turn("A", "VAR")
                pe.wait_ge(centred_squares, 4)
                token_sums([centred_sq[:, j, :] for j in range(CT)], K_MEAN_C, 4)

            def layer_norm_row():
                next_turn("A", "ROW")
                pe.wait_ge(inverse_ready, 2 * PAIRS + 2)
                spread_cols(turn, rms_col).then_inc(turn_made, 1)

            def acc_of(group):
                pe.wait_ge(emptied, group - 1)
                return acc[:, 2 * (group % 2):2 * (group % 2) + 2, :]

            for s in range(8):
                attention_slot("A", 3, s)
                if s == 0:
                    pe.wait_ge(mix_low_ready, 2)
                multiply(A0 + s, s, acc_of(GA + s), *h_tiles(2 * KC), True, True,
                         middle={2: layer_norm_mean, 4: layer_norm_variance, 5: layer_norm_row}.get(s))

            for n in range(8):
                dst = acc_of(GB + n)
                for b in range(3):
                    c = B0 + 3 * n + b
                    if n == 0:
                        for s in ((8,), (9,), (10, 11))[b]:
                            attention_slot("A", 3, s)
                        pe.wait_ge(mix_low_ready, (4, 6, 8)[b])
                    multiply(c, c, dst, *h_tiles(B_TILES[b]), b == 0, b == 2)

            def ffn_slot(g, s, c):
                if s % 4 == 0 and not 8 <= s < 16:
                    pe.wait_ge(emptied, up_group(g, (s if s < 8 else s - 8) // 4) - 1)
                if 8 <= s < 16:
                    if s == 8:
                        pe.wait_ge(hid_low_ready, 2 * g)
                    pe.wait_ge(emptied, down_group(g - 1, s - 8) - 1)
                    multiply(c, s, acc[:, 2 * (s % 2):2 * (s % 2) + 2, :], lambda j: hid_high[:, j, :],
                             lambda j: hid_low[:, j, :], True, True)
                    return
                tile0, pair = KC * (s % 4), (s // 4) % 2
                ready = None
                if isinstance(g, int) and s < 4:
                    def ready(j, tile0=tile0):
                        pe.wait_ge(h2_low_ready, tile0 + j + 1)
                multiply(c, s, acc[:, 2 * pair:2 * pair + 2, :], lambda j: h2_high[:, tile0 + j, :],
                         lambda j: h2_low[:, tile0 + j, :], s % 4 == 0, s % 4 == 3, ready)

            for l, s in enumerate(FIRST_SLOTS):
                if l == 2:
                    next_turn("F", "COL")
                    pe.wait_ge(res_squares_added, 8)
                    token_sums([square_sum[:, 0, :], square_sum[:, 1, :]], K_MEAN_D, 4)
                if l == 3:
                    next_turn("F", "ROW")
                    pe.wait_ge(inverse_ready, 2 * PAIRS + 3)
                    spread_cols(turn, rms_col).then_inc(turn_made, 1)
                ffn_slot(0, s, F0 + l)
            with pe.Fori(1, GROUPS) as g:
                for s in range(F_SLOTS):
                    ffn_slot(g, s, F_SLOTS * g + (F1 - F_SLOTS + s))
            for n in range(8):
                ffn_slot(GROUPS, 8 + n, LAST + n)


def needs_wait(i):
    return not (isinstance(i, int) and i == 0)


def constant_table():
    con = np.zeros((P, K_ALL), np.float32)
    con[:, K_ID:K_ID + P] = np.eye(P)
    offset = np.arange(BIAS_W)[None, :] - (S - P) - np.arange(P)[:, None]
    count = sum(((np.abs(offset) <= w // 2) & (offset % d == 0)).astype(int) for w, d in PATTERNS)
    con[:, K_DIST:K_DIST + BIAS_W] = np.abs(offset)
    con[:, K_LOGN:K_LOGN + BIAS_W] = np.where(count > 0, np.log(np.maximum(count, 1)), -1e30)
    con[:, K_MEAN_D] = 1 / D
    con[:, K_MEAN_C] = 1 / (CT * P)
    con[:, K_MEAN_H] = 1 / P
    con[:, K_EPS_R] = 1e-6
    con[:, K_EPS_L] = 1e-5
    con[:, K_SLOPE:K_SLOPE + HEADS] = [-2.0 ** (-8.0 * (h + 1) / HEADS) for h in range(HEADS)]
    return con


def channel_major(a):
    a = np.ascontiguousarray(a)
    a = a.reshape(1, -1) if a.ndim == 1 else a
    k, n = a.shape
    return a.reshape(k, n // P, P).transpose(2, 1, 0).reshape(P, -1)


def kernel(x, norm1_g, w_in, conv_dw_w, conv_dw_b, conv_ln_g, conv_ln_b, q_norm_g, k_norm_g, w_out, norm2_g,
           w_up, ffn_dw_w, ffn_dw_b, w_down):
    import concourse.bacc as bacc
    from concourse.bass_utils import run_bass_kernel_spmd

    params = np.concatenate([channel_major(a) for a in (
        norm1_g, norm2_g, conv_dw_w, conv_dw_b, conv_ln_g, conv_ln_b, q_norm_g, k_norm_g, ffn_dw_w, ffn_dw_b)], axis=1)
    arrays = {
        "x_t": np.ascontiguousarray(np.asarray(x)[0].T.reshape(DT, P, S).transpose(1, 0, 2)),
        "w_in": np.ascontiguousarray(w_in),
        "w_out": np.ascontiguousarray(w_out),
        "w_up": np.ascontiguousarray(w_up),
        "w_down": np.ascontiguousarray(w_down),
        "params": np.ascontiguousarray(params),
        "consts": constant_table(),
    }
    nc = bacc.Bacc("TRN2", target_bir_lowering=False, num_devices=1, dynamic_dma_scratch_size=1024)
    args = [nc.dram_tensor(f"{n}_dram", a.shape, F32, kind="ExternalInput").ap() for n, a in arrays.items()]
    out = nc.dram_tensor("out_dram", (P, DT, S), F32, kind="ExternalOutput").ap()
    hybrid_encoder_layer(nc, *args, out)
    result = run_bass_kernel_spmd(nc, [{f"{n}_dram": a for n, a in arrays.items()}], core_ids=[0])
    y = result.results[0]["out_dram"]
    return np.ascontiguousarray(y.transpose(1, 0, 2).reshape(D, S).T)[None]
```

```python
from contextlib import ExitStack

import numpy as np

import concourse.bass as bass
from concourse import mybir

ALU = mybir.AluOpType
ACT = mybir.ActivationFunctionType
F32 = mybir.dt.float32
F32R = mybir.dt.float32r
FLOAT_MAX = 3.0e38

P = 128
S = 512
QT = S // P
D = 2048
DT = D // P
CT = DT // 2
HEADS = 8
TAPS = 31
PAD = TAPS // 2
F = 5632
FT = F // P
KC = 4
NC = 2 * P
PAIRS = CT // 2
GROUPS = FT // KC
PATTERNS = ((128, 1), (512, 4), (2048, 16))

I_SLOTS = 20
A0 = I_SLOTS * PAIRS
B0 = A0 + D // NC
C0 = B0 + 2 * (D // NC)
F0 = C0 + D // NC
F1 = F0 + 16
F_SLOTS = 24
LAST = F1 + F_SLOTS * (GROUPS - 2)
SLOTS = LAST + F_SLOTS + 8

GA = 5 * PAIRS
GB = GA + D // NC
GC = GB + D // NC
GF = GC + D // NC

C_G1 = 0
C_G2 = C_G1 + DT
C_CW = C_G2 + DT
C_CB = C_CW + CT * TAPS
C_LG = C_CB + CT
C_LB = C_LG + CT
C_QG = C_LB + CT
C_KG = C_QG + 1
C_FW = C_KG + 1
C_FB = C_FW + 2 * FT * 3
C_ALL = C_FB + 2 * FT

BIAS_W = 2 * S - P
K_ID = 0
K_DIST = K_ID + P
K_LOGN = K_DIST + BIAS_W
K_MEAN_D = K_LOGN + BIAS_W
K_MEAN_C = K_MEAN_D + 1
K_MEAN_H = K_MEAN_C + 1
K_EPS_R = K_MEAN_H + 1
K_EPS_L = K_EPS_R + 1
K_SLOPE = K_EPS_L + 1
K_ALL = K_SLOPE + HEADS

T_FIRST = ["XCOL", "XROW", "Q", "K"]
T_PAIR = ["V0", "V1"] + [f"P{u}" for u in range(8)] + ["Q", "K"]
T_NORM = ["MU", "VAR", "ROW"]
T_LAST = T_PAIR[:10]
T_FFN = ["COL", "ROW"]


def t_use(i, name):
    if isinstance(i, str):
        uses = {"A": T_NORM, "B": T_LAST, "F": T_FFN}
        before = len(T_FIRST) + (PAIRS - 1) * len(T_PAIR) + sum(len(uses[k]) for k in uses if k < i)
        return before + uses[i].index(name) + 1
    if isinstance(i, int) and i == 0:
        return T_FIRST.index(name) + 1
    return len(T_PAIR) * i + (len(T_FIRST) - len(T_PAIR) + T_PAIR.index(name) + 1)


def taps_of(slot):
    count = {9: 4, 10: 6, 11: 6, 12: 3, 13: 6, 14: 6, 15: 6, 16: 3, 17: 5, 18: 5, 19: 2}
    late = {0: 3, 1: 3, 2: 2, 3: 2}
    at = 0
    for s in sorted(count):
        if s == slot:
            return range(at, at + count[s])
        at += count[s]
    for s in sorted(late):
        if s == slot:
            return range(at, at + late[s])
        at += late[s]
    assert at == 2 * TAPS
    return range(0)


def hybrid_encoder_layer(nc, x_t, w_in, w_out, w_up, w_down, params, consts, out):
    with ExitStack() as ctx:
        def sem(name):
            return ctx.enter_context(nc.semaphore(name))

        start = -(-nc.sbuf_base // 32) * 32

        def place(name, shape, dt, offset):
            size = 4 * int(np.prod(shape[1:]))
            assert offset % 32 == 0 and start + offset + size <= nc.sbuf_usable_end, name
            return nc.alloc_sbuf_tensor_at(name, shape, dt, offset=start + offset), -(-(offset + size) // 32) * 32

        par, o = place("channel_params", [P, C_ALL], F32, 0)
        con, o = place("constants", [P, K_ALL], F32, o)
        qk_gain, o = place("qk_gain", [P, 1], F32, o)
        mean_sq, o = place("mean_sq", [P, 8], F32, o)
        std_col, o = place("std_col", [P, 8], F32, o)
        wait_cell, o = place("wait_cell", [P, 1], F32, o)
        newton, o = place("newton", [P, 8], F32, o)
        rms_col, o = place("rms_col", [P, 4], F32, o)
        rq_col, o = place("rq_col", [P, 8], F32, o)
        rk_col, o = place("rk_col", [P, 8], F32, o)
        neg_max, o = place("neg_max", [P, 2], F32, o)
        row_sum, o = place("row_sum", [P, 2], F32, o)
        row_inv, o = place("row_inv", [P, 2], F32, o)
        rms_row, o = place("rms_row", [P, S], F32, o)
        w_raw, o = place("w_raw", [P, 4, KC * NC], F32, o)
        w_high, o = place("w_high", [P, 2, KC * NC], F32R, o)
        w_low, o = place("w_low", [P, 2, KC * NC], F32R, o)
        squares, o = place("squares", [P, 2, S], F32, o)
        ln_mean, ln_rstd = squares[:, 0, :], squares[:, 1, :]
        square_sum, o = place("square_sum", [P, 2, S], F32, o)
        conv_sum = square_sum[:, 0, :]
        res, o = place("residual", [P, DT, S], F32, o)
        r1 = o
        h_high, o = place("h_high", [P, DT, S], F32R, r1)
        h_low, o = place("h_low", [P, DT, S], F32R, o)
        centred_sq, _ = place("centred_sq", [P, CT, S], F32, r1)
        hid_high, f = place("hid_high", [P, KC, S], F32R, r1)
        hid_low, f = place("hid_low", [P, KC, S], F32R, f)
        last_high, f = place("last_high", [P, KC, S], F32R, f)
        last_low, f = place("last_low", [P, KC, S], F32R, f)
        gated, f = place("gated", [P, KC, S], F32, f)
        up_pad, f = place("up_pad", [P, 2, S + 2], F32, f)
        up_conv, f = place("up_conv", [P, 2, S], F32, f)
        assert f <= o
        r2 = o
        mixed, o = place("mixed", [P, DT, S], F32, r2)
        q_t, o = place("q_t", [P, 2, S], F32, o)
        k_t, o = place("k_t", [P, 2, S], F32, o)
        early_high, e = place("early_high", [P, KC, S], F32R, o)
        early_low, e = place("early_low", [P, KC, S], F32R, e)
        v_n, o = place("v_n", [P, 2, S], F32, o)
        probs, o = place("probs", [P, 2, S], F32, o)
        probs_t, o = place("probs_t", [P, 2, S], F32, o)
        o = max(o, e)
        bias, o = place("bias", [P, BIAS_W], F32, o)
        glu, o = place("glu", [P, 2, S + 2 * PAD], F32, o)
        h2_high, g = place("h2_high", [P, DT, S], F32R, r2)
        h2_low, g = place("h2_low", [P, DT, S], F32R, g)

        acc = ctx.enter_context(nc.psum_tensor("acc", [P, 4, S], F32))
        score = ctx.enter_context(nc.psum_tensor("score", [P, 2, S], F32))
        turn = ctx.enter_context(nc.psum_tensor("turn", [P, S], F32))
        attn_o = ctx.enter_context(nc.psum_tensor("attn_o", [P, S], F32))

        ident = con[:, K_ID:K_ID + P]

        def const_col(c):
            return con[:, c:c + 1]

        def param(c):
            return par[:, bass.ds(c, 1)]

        params_in, const_in = sem("params_in"), sem("const_in")
        x_in = [sem(f"x_in{k}") for k in range(4)]
        w_arrived = [sem(f"w_arrived{k}") for k in range(4)]
        w_high_ready, w_low_ready, chunk_done = sem("w_high_ready"), sem("w_low_ready"), sem("chunk_done")
        x_high_ready, x_low_ready = sem("x_high_ready"), sem("x_low_ready")
        squares_ready, squares_added = sem("squares_ready"), sem("squares_added")
        emptied = sem("emptied")
        turn_made, turn_read = sem("turn_made"), sem("turn_read")
        x0_in = [sem(f"x0_in{j}") for j in range(KC)]
        std_ready, newton_step = sem("std_ready"), sem("newton_step")
        inverse_ready, gain_ready, pads_ready, sum_cleared = (sem(n) for n in (
            "inverse_ready", "gain_ready", "pads_ready", "sum_cleared"))
        sigmoid_ready, glu_ready, tap_done, conv_added = (sem(n) for n in (
            "sigmoid_ready", "glu_ready", "tap_done", "conv_added"))
        head_squares, k_spread, k_ready = sem("head_squares"), sem("k_spread"), sem("k_ready")
        bias_ready, score_made, score_read, max_ready, exp_done, sum_inverted, probs_ready, pv_done, o_read = (
            sem(n) for n in ("bias_ready", "score_made", "score_read", "max_ready", "exp_done",
                             "sum_inverted", "probs_ready", "pv_done", "o_read"))
        centred, centred_squares, centred_added, scaled, conv_out = (sem(n) for n in (
            "centred", "centred_squares", "centred_added", "scaled", "conv_out"))
        mix_high_ready, mix_low_ready = sem("mix_high_ready"), sem("mix_low_ready")
        h2_high_ready, h2_low_ready, res_squares, res_squares_added = (sem(n) for n in (
            "h2_high_ready", "h2_low_ready", "res_squares", "res_squares_added"))
        ffn_pads, up_mid, up_side, gate_act, hidden_ready, hid_high_ready, hid_low_ready = (sem(n) for n in (
            "ffn_pads", "up_mid", "up_side", "gate_act", "hidden_ready", "hid_high_ready", "hid_low_ready"))
        out_written = sem("out_written")

        def weight_slab(w, tile0, col):
            rows = w.rearrange("(t p) n -> p t n", p=P)
            return rows[:, bass.ds(tile0, KC), bass.ds(col, NC)]

        def in_slab(i, s):
            return weight_slab(w_in, KC * (s % 4), 4 * NC * (s // 4) + NC * i)

        def ffn_slab(g, s):
            if s < 8:
                return weight_slab(w_up, KC * (s % 4), KC * P * g + NC * (s // 4))
            if s < 16:
                return weight_slab(w_down, KC * (g - 1), NC * (s - 8))
            return weight_slab(w_up, KC * (s % 4), KC * P * g + (F + NC * ((s - 16) // 4)))

        FIRST_SLOTS = [*range(8), *range(16, F_SLOTS)]

        def up_group(g, y):
            if isinstance(g, int) and g in (0, GROUPS - 1):
                return (GF if g == 0 else 12 * (GROUPS - 2) + GF + 4) + y
            return 12 * g + (GF - 8 + (y if y < 2 else y + 8))

        def down_group(g, n):
            if isinstance(g, int) and g >= GROUPS - 2:
                return 12 * (GROUPS - 2) + (GF + 8 + 8 * (g - GROUPS + 2) + n)
            return 12 * g + (GF + 6 + n)

        block = ctx.enter_context(nc.Block())

        @block.sync
        def _(sp):
            def fetch(c, s, slab, wait=True):
                if wait:
                    sp.wait_ge(w_low_ready, c - 3)
                sp.dma_start(w_raw[:, s % 4, :].rearrange("p (t n) -> p t n", n=NC), slab).then_inc(
                    w_arrived[s % 4], 16)

            sp.dma_start(par[:], params).then_inc(params_in, 16)
            for j in range(KC):
                sp.dma_start(res[:, j, :], x_t[:, j, :]).then_inc(x0_in[j], 16)
                if j == 0:
                    fetch(0, 0, in_slab(0, 0), wait=False)
            for k in range(1, 4):
                sp.dma_start(res[:, KC * k:KC * (k + 1), :], x_t[:, KC * k:KC * (k + 1), :]).then_inc(x_in[k], 16)
                fetch(k, k, in_slab(0, k), wait=False)
            sp.dma_start(con[:], consts).then_inc(const_in, 16)
            for s in range(4, I_SLOTS):
                fetch(s, s, in_slab(0, s))
            with sp.Fori(1, PAIRS) as i:
                for s in range(I_SLOTS):
                    fetch(I_SLOTS * i + s, s, in_slab(i, s))
            for n in range(8):
                fetch(A0 + n, A0 + n, weight_slab(w_out, 2 * KC, NC * n))
            for n in range(8):
                for b in range(2):
                    fetch(B0 + 2 * n + b, 2 * n + b, weight_slab(w_out, KC * b, NC * n))
            for n in range(8):
                fetch(C0 + n, n, weight_slab(w_out, 3 * KC, NC * n))
            for l, s in enumerate(FIRST_SLOTS):
                fetch(F0 + l, l, ffn_slab(0, s))
            with sp.Fori(1, GROUPS - 1) as g:
                for s in range(F_SLOTS):
                    fetch(F_SLOTS * g + (F1 - F_SLOTS + s), s, ffn_slab(g, s))
            for l, s in enumerate(FIRST_SLOTS):
                fetch(LAST + l, l, ffn_slab(GROUPS - 1, s))
            for l in range(16):
                fetch(LAST + 16 + l, l, ffn_slab(GROUPS - 1 + l // 8, 8 + l % 8))
            for n in range(8):
                sp.wait_ge(emptied, down_group(GROUPS - 1, n) + 1)
                sp.dma_start(out[:, 2 * n:2 * n + 2, :], res[:, 2 * n:2 * n + 2, :]).then_inc(out_written, 16)
            sp.wait_ge(out_written, 16 * 8)

        @block.gpsimd
        def _(pool):
            pool.wait_ge(turn_made, t_use(0, "XCOL"))
            nc.gpsimd.memset(conv_sum, 0.0).then_inc(sum_cleared, 1)

            def add_tile(i, t):
                first = isinstance(i, int) and t == 0
                if first:
                    pool.wait_ge(sum_cleared, 1)
                else:
                    pool.wait_ge(conv_added, 2 * i + t)
                if t == 0:
                    pool.wait_ge(tap_done, 2 * TAPS * i + 2 * TAPS)
                nc.gpsimd.tensor_tensor(conv_sum.rearrange("p (o n) -> p o n", o=1),
                                        conv_sum.rearrange("p (o n) -> p o n", o=1),
                                        mixed[:, bass.ds(2 * i + t, 1), :], ALU.add).then_inc(conv_added, 1)

            add_tile(0, 0)
            add_tile(0, 1)
            with pool.Fori(1, PAIRS) as i:
                add_tile(i, 0)
                add_tile(i, 1)

        @block.scalar
        def _(act):
            def split_high(c, s, buffer_used=True):
                act.wait_ge(w_arrived[s % 4], 4 * (c - s % 4) + 16)
                if buffer_used:
                    act.wait_ge(chunk_done, c - 1)
                nc.scalar.activation(w_high[:, s % 2, :], w_raw[:, s % 4, :], ACT.Copy).then_inc(w_high_ready, 1)

            def x_chunk(k):
                if k:
                    act.wait_ge(x_in[k], 16)
                for j in range(KC * k, KC * (k + 1)):
                    if k == 0:
                        act.wait_ge(x0_in[j], 16)
                    nc.scalar.activation(h_high[:, j, :], res[:, j, :], ACT.Copy, scale=param(C_G1 + j)
                                         ).then_inc(x_high_ready, 1)
                    if j == 0:
                        split_high(0, 0, buffer_used=False)
                if k == 0:
                    split_high(1, 1, buffer_used=False)
                for n in range(2 * k, 2 * k + 2):
                    if n:
                        act.wait_ge(squares_added, n)
                    nc.scalar.activation(squares[:], res[:, 2 * n:2 * n + 2, :], ACT.Square).then_inc(squares_ready, 1)

            def turn_copy(i, name, dst):
                act.wait_ge(turn_made, t_use(i, name))
                nc.scalar.activation(dst, turn[:], ACT.Copy).then_inc(turn_read, 1)

            def turn_sqrt(i, name, n, width, eps):
                act.wait_ge(turn_made, t_use(i, name))
                nc.scalar.activation(mean_sq[:, 0:width], turn[:, 0:width], ACT.Identity, bias=const_col(eps)
                                     ).then_inc(turn_read, 1)
                act.wait_ge(turn_read, t_use(i, name))
                nc.scalar.activation(std_col[:, 0:width], mean_sq[:, 0:width], ACT.Sqrt).then_inc(std_ready, 1)

            def scale_unit(i, j, u):
                act.wait_ge(score_made, 8 * j + (u + 1))
                if u >= 2:
                    act.wait_ge(turn_made, t_use(i, f"P{u - 2}"))
                nc.scalar.activation(probs[:, u % 2, :], score[:, u % 2, :], ACT.Copy, scale=rq_col[:, u:u + 1]
                                     ).then_inc(score_read, 1)

            def exp_unit(j, u):
                act.wait_ge(max_ready, 8 * j + (u + 1))
                nc.scalar.activation(probs[:, u % 2, :], probs[:, u % 2, :], ACT.Exp, bias=neg_max[:, u % 2:u % 2 + 1],
                                     scale=-1.0, accum_out=row_sum[:, u % 2:u % 2 + 1]).then_inc(exp_done, 1)

            def normalise_unit(j, u):
                act.wait_ge(sum_inverted, 8 * j + (u + 1))
                nc.scalar.activation(probs[:, u % 2, :], probs[:, u % 2, :], ACT.Copy,
                                     scale=row_inv[:, u % 2:u % 2 + 1]).then_inc(probs_ready, 1)

            def attention_slot(i, j, s):
                if s in (1, 2):
                    turn_copy(i, f"V{s - 1}", v_n[:, s - 1, :])
                if 3 <= s <= 10:
                    u = s - 3
                    if u >= 2:
                        act.wait_ge(pv_done, 8 * j + (u - 1))
                    turn_copy(i, f"P{u}", probs_t[:, u % 2, :])
                if s == 1:
                    act.wait_ge(inverse_ready, 2 * j + 2)
                if 1 <= s <= 8:
                    scale_unit(i, j, s - 1)
                if 2 <= s <= 9:
                    normalise_unit(j, s - 2)
                if 1 <= s <= 8:
                    exp_unit(j, s - 1)
                if s in (7, 11):
                    hh = s // 11
                    act.wait_ge(pv_done, 8 * j + (4 * hh + 4))
                    nc.scalar.activation(mixed[:, bass.ds(2 * j + (CT + hh), 1), :], attn_o[:].rearrange(
                        "p (o n) -> p o n", o=1), ACT.Copy).then_inc(o_read, 1)

            def iteration(i):
                first = isinstance(i, int)
                c0 = I_SLOTS * i
                for s in range(I_SLOTS):
                    if not (first and s == 0):
                        split_high(c0 + (s + 1), s + 1)
                    if first and s < 3:
                        x_chunk(s + 1)
                    if first and s == 5:
                        turn_sqrt(0, "XCOL", 1, 4, K_EPS_R)
                    if first and s == 6:
                        turn_copy(0, "XROW", rms_row[:])
                    if not first:
                        attention_slot(i, i - 1, s)
                    if s == 8:
                        act.wait_ge(emptied, 5 * i + 2)
                        nc.scalar.activation(q_t[:], q_t[:], ACT.Sigmoid).then_inc(sigmoid_ready, 1)
                    if s == 12:
                        act.wait_ge(emptied, 5 * i + 3)
                        nc.scalar.activation(squares[:], q_t[:], ACT.Square).then_inc(head_squares, 1)
                    if s == 14:
                        turn_sqrt(i, "Q", 2 * i + 2, 8, K_EPS_R)
                    if s == 16:
                        act.wait_ge(emptied, 5 * i + 4)
                        act.wait_ge(turn_made, t_use(i, "Q"))
                        nc.scalar.activation(squares[:], k_t[:], ACT.Square).then_inc(head_squares, 1)
                    if s == 17:
                        act.wait_ge(inverse_ready, 2 * i + 2)
                        turn_sqrt(i, "K", 2 * i + 3, 8, K_EPS_R)

            def mix_high(pair):
                nc.scalar.activation(h_high[:, 2 * pair:2 * pair + 2, :], mixed[:, 2 * pair:2 * pair + 2, :],
                                     ACT.Copy).then_inc(mix_high_ready, 1)

            act.wait_ge(params_in, 16)
            x_chunk(0)
            iteration(0)
            with act.Fori(1, PAIRS) as i:
                iteration(i)

            act.wait_ge(o_read, 6)
            for n in range(2):
                nc.scalar.activation(early_high[:, 2 * n:2 * n + 2, :], mixed[:, CT + 2 * n:CT + 2 * n + 2, :],
                                     ACT.Copy).then_inc(mix_high_ready, 1)

            for s in range(8):
                if s < 7:
                    split_high(A0 + s + 1, s + 1)
                if s == 2:
                    turn_copy("A", "MU", ln_mean)
                if s == 3:
                    act.wait_ge(chunk_done, A0)
                    for n in range(4):
                        act.wait_ge(centred, n + 1)
                        nc.scalar.activation(centred_sq[:, 2 * n:2 * n + 2, :], mixed[:, 2 * n:2 * n + 2, :],
                                             ACT.Square).then_inc(centred_squares, 1)
                if s == 5:
                    turn_sqrt("A", "VAR", 2 * PAIRS + 2, 4, K_EPS_L)
                if s == 6:
                    turn_copy("A", "ROW", ln_rstd)
                    for n in range(4):
                        act.wait_ge(scaled, n + 1)
                        for j in (2 * n, 2 * n + 1):
                            nc.scalar.activation(mixed[:, j, :], mixed[:, j, :], ACT.Silu, scale=param(C_LG + j),
                                                 bias=param(C_LB + j)).then_inc(conv_out, 1)
                        act.wait_ge(conv_out, 2 * n + 2)
                        mix_high(n)
                        if n == 1:
                            split_high(A0 + 8, 0)

            def h2_high_pair(n):
                act.wait_ge(emptied, GC + n + 1)
                for j in (2 * n, 2 * n + 1):
                    nc.scalar.activation(h2_high[:, j, :], res[:, j, :], ACT.Copy, scale=param(C_G2 + j)
                                         ).then_inc(h2_high_ready, 1)
                if n:
                    act.wait_ge(res_squares_added, n)
                nc.scalar.activation(squares[:], res[:, 2 * n:2 * n + 2, :], ACT.Square).then_inc(res_squares, 1)

            for s in range(16):
                split_high(B0 + s + 1, s + 1)
                attention_slot("B", PAIRS - 1, s)
                if s == 12:
                    act.wait_ge(o_read, HEADS)
                    mix_high(6)
                    mix_high(7)

            for n in range(8):
                split_high(C0 + n + 1, n + 1)
                if n == 1:
                    act.wait_ge(mix_low_ready, 8)
                if n:
                    h2_high_pair(n - 1)

            def up_act(g, y):
                act.wait_ge(emptied, up_group(g, y) + 1)
                if y == 0 and needs_wait(g):
                    act.wait_ge(hidden_ready, 2 * g)
                if y == 3:
                    act.wait_ge(hidden_ready, 2 * g + 1)
                for t in range(2):
                    f = FT * (y // 2) + 2 * (y % 2) + t
                    nc.scalar.activation(up_conv[:, t, :], up_pad[:, t, 1:S + 1], ACT.Identity,
                                         scale=param(3 * KC * g + (C_FW + 3 * f + 1)),
                                         bias=param(KC * g + (C_FB + f))).then_inc(up_mid, 1)

            def gate_swish(g, y):
                act.wait_ge(up_side, 16 * g + (4 * y + 4))
                if needs_wait(g):
                    act.wait_ge(hid_low_ready, 2 * g + (y - 1))
                nc.scalar.activation(gated[:, 2 * y:2 * y + 2, :], up_conv[:], ACT.Silu).then_inc(gate_act, 1)

            def hidden_high(g, y):
                act.wait_ge(hidden_ready, 2 * g + (y + 1))
                high = hid_high
                if is_last(g):
                    high = last_high
                elif y == 0 and needs_wait(g):
                    act.wait_ge(chunk_done, F_SLOTS * g + (F1 - F_SLOTS + 16))
                nc.scalar.activation(high[:, 2 * y:2 * y + 2, :], gated[:, 2 * y:2 * y + 2, :], ACT.Copy
                                     ).then_inc(hid_high_ready, 1)

            def ffn_slot(g, s, c):
                first = isinstance(g, int)
                split_high(c + 1, c + 1 if first else s + 1)
                if s == 0 and needs_wait(g):
                    up_act(g - 1, 3)
                if s == 2 and needs_wait(g):
                    hidden_high(g - 1, 1)
                if s == 4:
                    up_act(g, 0)
                if s == 5:
                    gate_swish(g, 0)
                if s == (16 if first else 8):
                    up_act(g, 1)
                if s == (17 if first else 9):
                    gate_swish(g, 1)
                if s == 20:
                    up_act(g, 2)
                if s == 22:
                    hidden_high(g, 0)

            for l, s in enumerate(FIRST_SLOTS):
                ffn_slot(0, s, F0 + l)
                if l == 0:
                    h2_high_pair(7)
                if l == 2:
                    turn_sqrt("F", "COL", 2 * PAIRS + 3, 4, K_EPS_R)
                if l == 3:
                    turn_copy("F", "ROW", rms_row[:])
            with act.Fori(1, GROUPS - 1) as g:
                for s in range(F_SLOTS):
                    ffn_slot(g, s, F_SLOTS * g + (F1 - F_SLOTS + s))
            for l, s in enumerate(FIRST_SLOTS):
                ffn_slot(GROUPS - 1, s, LAST + l)
            for l in range(16):
                if l < 15:
                    split_high(LAST + l + 17, l + 17)
                if l == 0:
                    up_act(GROUPS - 1, 3)
                if l == 2:
                    hidden_high(GROUPS - 1, 1)

        @block.vector
        def _(dve):
            v = nc.vector

            def split_low(c, s):
                dve.wait_ge(w_high_ready, c + 1)
                v.tensor_tensor(w_low[:, s % 2, :], w_raw[:, s % 4, :], w_high[:, s % 2, :].bitcast(F32),
                                ALU.subtract).then_inc(w_low_ready, 1)

            def add_squares(n, ready, added):
                dve.wait_ge(ready, n + 1)
                if n == 0:
                    v.tensor_copy(square_sum[:], squares[:]).then_inc(added, 1)
                else:
                    dve.wait_ge(added, n)
                    v.tensor_tensor(square_sum[:], square_sum[:], squares[:], ALU.add).then_inc(added, 1)

            def x_chunk(k):
                for j in range(KC * k, KC * (k + 1)):
                    dve.wait_ge(x_high_ready, j + 1)
                    v.scalar_tensor_tensor(out=h_low[:, j, :], in0=res[:, j, :], scalar=param(C_G1 + j),
                                           in1=h_high[:, j, :].bitcast(F32), op0=ALU.mult, op1=ALU.subtract
                                           ).then_inc(x_low_ready, 1)
                    if j == 0:
                        split_low(0, 0)
                if k == 0:
                    split_low(1, 1)
                for n in range(2 * k, 2 * k + 2):
                    add_squares(n, squares_ready, squares_added)

            def spread(row):
                return row.rearrange("p (o n) -> p o n", o=1).broadcast_to([P, 2, S])

            def scale_out(c_done, src, dst):
                dve.wait_ge(chunk_done, c_done)
                v.tensor_tensor(dst, src, spread(rms_row[:]), ALU.mult).then_inc(emptied, 1)

            def invert(name, n, dst, width):
                r, step, mean = dst[:, 0:width], newton[:, 0:width], mean_sq[:, 0:width]
                dve.wait_ge(std_ready, n)
                v.reciprocal(r, std_col[:, 0:width]).then_inc(newton_step, 1)
                dve.wait_ge(newton_step, 4 * n - 3)
                v.tensor_tensor(step, r, r, ALU.mult).then_inc(newton_step, 1)
                dve.wait_ge(newton_step, 4 * n - 2)
                v.tensor_tensor(step, step, mean, ALU.mult).then_inc(newton_step, 1)
                dve.wait_ge(newton_step, 4 * n - 1)
                v.tensor_scalar(step, step, -0.5, 1.5, ALU.mult, ALU.add).then_inc(newton_step, 1)
                dve.wait_ge(newton_step, 4 * n)
                v.tensor_tensor(r, r, step, ALU.mult).then_inc(inverse_ready, 1)

            def taps(i, steps):
                for m in steps:
                    k, t = m // 2, m % 2
                    y = mixed[:, bass.ds(2 * i + t, 1), :]
                    src = glu[:, t:t + 1, k:k + S]
                    w = param(2 * TAPS * i + (C_CW + TAPS * t + k))
                    if k == 0:
                        v.tensor_scalar(y, src, w, param(2 * i + (C_CB + t)), ALU.mult, ALU.add).then_inc(tap_done, 1)
                    else:
                        dve.wait_ge(tap_done, 2 * TAPS * i + (m - 1))
                        v.scalar_tensor_tensor(out=y, in0=src, scalar=w, in1=y, op0=ALU.mult, op1=ALU.add
                                               ).then_inc(tap_done, 1)

            def bias_table(j, hh):
                v.scalar_tensor_tensor(out=bias[:], in0=con[:, K_DIST:K_DIST + BIAS_W],
                                       scalar=con[:, bass.ds(2 * j + (K_SLOPE + hh), 1)],
                                       in1=con[:, K_LOGN:K_LOGN + BIAS_W], op0=ALU.mult, op1=ALU.add
                                       ).then_inc(bias_ready, 1)

            def score_unit(j, u):
                dve.wait_ge(score_read, 8 * j + (u + 1))
                dve.wait_ge(bias_ready, 2 * j + (u // 4 + 1))
                v.memset(wait_cell[:], 0.0)
                x0 = P * (QT - 1 - u % QT)
                v.tensor_tensor_reduce(probs[:, u % 2, :], probs[:, u % 2, :], bias[:, x0:x0 + S], -1.0, FLOAT_MAX,
                                       ALU.add, ALU.min, neg_max[:, u % 2:u % 2 + 1]).then_inc(max_ready, 1)

            def invert_sum(j, u):
                dve.wait_ge(exp_done, 8 * j + (u + 1))
                v.reciprocal(row_inv[:, u % 2:u % 2 + 1], row_sum[:, u % 2:u % 2 + 1]).then_inc(sum_inverted, 1)

            def attention_slot(j, s):
                if 2 <= s <= 9:
                    invert_sum(j, s - 2)
                if s == 0:
                    bias_table(j, 0)
                if s == 5:
                    bias_table(j, 1)
                if 1 <= s <= 8:
                    score_unit(j, s - 1)

            def v_out(i):
                scale_out(I_SLOTS * i + I_SLOTS, score[:], mixed[:, DT - 2:DT, :])

            def iteration(i):
                first = isinstance(i, int)
                c0 = I_SLOTS * i
                for s in range(I_SLOTS):
                    if s == 0 and not first:
                        v_out(i - 1)
                    if s == (7 if first else 4):
                        if first:
                            dve.wait_ge(turn_read, t_use(0, "XROW"))
                        scale_out(c0 + 4, acc[:, 0:2, :], mixed[:, bass.ds(2 * i, 2), :])
                    if s == 8:
                        if not first:
                            dve.wait_ge(score_made, 8 * i)
                        scale_out(c0 + 8, acc[:, 2:4, :], q_t[:])
                    if s == 12:
                        scale_out(c0 + 12, acc[:, 0:2, :], q_t[:])
                    if s == 15:
                        invert("Q", 2 * i + 2, rq_col, 8)
                    if s == 16:
                        scale_out(c0 + 16, acc[:, 2:4, :], k_t[:])
                    if s == 18:
                        invert("K", 2 * i + 3, rk_col, 8)
                    if not (first and s == 0):
                        split_low(c0 + (s + 1), s + 1)
                    if first and s < 3:
                        x_chunk(s + 1)
                    if first and s == 5:
                        invert("XCOL", 1, rms_col, 4)
                    if not first:
                        attention_slot(i - 1, s)
                        if s < 4:
                            taps(i - 1, taps_of(s))
                    if s == 9:
                        dve.wait_ge(sigmoid_ready, i + 1)
                        if first:
                            dve.wait_ge(pads_ready, 2)
                        v.tensor_tensor(glu[:, :, PAD:PAD + S], mixed[:, bass.ds(2 * i, 2), :], q_t[:], ALU.mult
                                        ).then_inc(glu_ready, 1)
                        dve.wait_ge(glu_ready, i + 1)
                    if s >= 9:
                        taps(i, taps_of(s))
                    if s == 19:
                        dve.wait_ge(k_spread, i + 1)
                        for hh, bank in ((0, turn), (1, attn_o)):
                            v.scalar_tensor_tensor(out=k_t[:, hh, :], in0=k_t[:, hh, :], scalar=qk_gain[:, 0:1],
                                                   in1=bank[:], op0=ALU.mult, op1=ALU.mult).then_inc(k_ready, 1)

            def mix_low(n, pair):
                dve.wait_ge(mix_high_ready, n + 3)
                v.tensor_tensor(h_low[:, 2 * pair:2 * pair + 2, :], mixed[:, 2 * pair:2 * pair + 2, :],
                                h_high[:, 2 * pair:2 * pair + 2, :].bitcast(F32), ALU.subtract
                                ).then_inc(mix_low_ready, 1)

            def res_add(n, group, c_done):
                dve.wait_ge(chunk_done, c_done)
                pair = group % 2 if isinstance(group, int) else n % 2
                v.tensor_tensor(res[:, 2 * n:2 * n + 2, :], res[:, 2 * n:2 * n + 2, :],
                                acc[:, 2 * pair:2 * pair + 2, :], ALU.add).then_inc(emptied, 1)

            v.memset(glu[:, :, 0:PAD], 0.0).then_inc(pads_ready, 1)
            v.memset(glu[:, :, PAD + S:], 0.0).then_inc(pads_ready, 1)
            dve.wait_ge(params_in, 16)
            v.scalar_tensor_tensor(out=qk_gain[:], in0=param(C_QG), scalar=float(P) ** -0.5, in1=param(C_KG),
                                   op0=ALU.mult, op1=ALU.mult).then_inc(gain_ready, 1)
            x_chunk(0)
            dve.wait_ge(gain_ready, 1)
            iteration(0)
            dve.wait_ge(const_in, 16)
            with dve.Fori(1, PAIRS) as i:
                iteration(i)

            for n in range(2):
                dve.wait_ge(mix_high_ready, n + 1)
                v.tensor_tensor(early_low[:, 2 * n:2 * n + 2, :], mixed[:, CT + 2 * n:CT + 2 * n + 2, :],
                                early_high[:, 2 * n:2 * n + 2, :].bitcast(F32), ALU.subtract
                                ).then_inc(mix_low_ready, 1)

            for s in range(8):
                if s == 0:
                    v_out(PAIRS - 1)
                else:
                    res_add(s - 1, GA + s - 1, A0 + s)
                split_low(A0 + s + 1, s + 1)
                if s < 2:
                    for late in (2 * s, 2 * s + 1):
                        taps(PAIRS - 1, taps_of(late))
                if s == 2:
                    dve.wait_ge(turn_read, t_use("A", "MU"))
                    for n in range(4):
                        v.tensor_tensor(mixed[:, 2 * n:2 * n + 2, :], mixed[:, 2 * n:2 * n + 2, :], spread(ln_mean),
                                        ALU.subtract).then_inc(centred, 1)
                if s == 3:
                    for n in range(1, 4):
                        dve.wait_ge(centred_squares, n + 1)
                        if n == 1:
                            v.tensor_tensor(square_sum[:], centred_sq[:, 0:2, :], centred_sq[:, 2:4, :], ALU.add
                                            ).then_inc(centred_added, 1)
                            continue
                        dve.wait_ge(centred_added, n - 1)
                        v.tensor_tensor(square_sum[:], square_sum[:], centred_sq[:, 2 * n:2 * n + 2, :], ALU.add
                                        ).then_inc(centred_added, 1)
                if s == 5:
                    invert("VAR", 2 * PAIRS + 2, rms_col, 4)
                if s == 6:
                    dve.wait_ge(turn_read, t_use("A", "ROW"))
                    for n in range(4):
                        v.tensor_tensor(mixed[:, 2 * n:2 * n + 2, :], mixed[:, 2 * n:2 * n + 2, :], spread(ln_rstd),
                                        ALU.mult).then_inc(scaled, 1)
                        if n:
                            mix_low(n - 1, n - 1)
                if s == 7:
                    mix_low(3, 3)

            def h2_low_pair(n):
                for j in (2 * n, 2 * n + 1):
                    dve.wait_ge(h2_high_ready, j + 1)
                    v.scalar_tensor_tensor(out=h2_low[:, j, :], in0=res[:, j, :], scalar=param(C_G2 + j),
                                           in1=h2_high[:, j, :].bitcast(F32), op0=ALU.mult, op1=ALU.subtract
                                           ).then_inc(h2_low_ready, 1)
                add_squares(n, res_squares, res_squares_added)

            for s in range(16):
                if s == 0:
                    res_add(7, GA + 7, B0)
                if s and s % 2 == 0:
                    res_add(s // 2 - 1, GB + s // 2 - 1, B0 + s)
                split_low(B0 + s + 1, s + 1)
                attention_slot(PAIRS - 1, s)
                if s == 12:
                    mix_low(4, 6)
                    mix_low(5, 7)

            for n in range(8):
                if n == 0:
                    res_add(7, GB + 7, C0)
                else:
                    res_add(n - 1, GC + n - 1, C0 + n)
                split_low(C0 + n + 1, n + 1)
                if n:
                    h2_low_pair(n - 1)

            def up_out(g, y, c_done):
                if y or needs_wait(g):
                    dve.wait_ge(up_mid, 8 * g + 2 * y)
                pair = y % 2
                scale_out(c_done, acc[:, 2 * pair:2 * pair + 2, :], up_pad[:, :, 1:S + 1])

            def up_taps(g, y):
                for k in (0, 2):
                    for t in range(2):
                        f = FT * (y // 2) + 2 * (y % 2) + t
                        if k == 0:
                            dve.wait_ge(up_mid, 8 * g + (2 * y + t + 1))
                        else:
                            dve.wait_ge(up_side, 16 * g + (4 * y + t + 1))
                        v.scalar_tensor_tensor(out=up_conv[:, t, :], in0=up_pad[:, t, k:k + S],
                                               scalar=param(3 * KC * g + (C_FW + 3 * f + k)), in1=up_conv[:, t, :],
                                               op0=ALU.mult, op1=ALU.add).then_inc(up_side, 1)

            def hidden(g, y):
                dve.wait_ge(up_side, 16 * g + (4 * y + 12))
                dve.wait_ge(gate_act, 2 * g + (y + 1))
                v.tensor_tensor(gated[:, 2 * y:2 * y + 2, :], gated[:, 2 * y:2 * y + 2, :], up_conv[:], ALU.mult
                                ).then_inc(hidden_ready, 1)

            def hidden_low(g, y):
                dve.wait_ge(hid_high_ready, 2 * g + (y + 1))
                high, low = (last_high, last_low) if is_last(g) else (hid_high, hid_low)
                v.tensor_tensor(low[:, 2 * y:2 * y + 2, :], gated[:, 2 * y:2 * y + 2, :],
                                high[:, 2 * y:2 * y + 2, :].bitcast(F32), ALU.subtract).then_inc(hid_low_ready, 1)

            def ffn_slot(g, s, c):
                first = isinstance(g, int)
                if s == 0 and needs_wait(g):
                    up_out(g - 1, 3, c)
                if s == 4:
                    if not needs_wait(g):
                        dve.wait_ge(turn_read, t_use("F", "ROW"))
                    up_out(g, 0, c)
                if s == (16 if first else 8):
                    up_out(g, 1, c)
                if 9 <= s <= 16 and not first:
                    res_add(s - 9, g, c)
                if s == 20:
                    up_out(g, 2, c)
                split_low(c + 1, c + 1 if first else s + 1)
                if s == 0 and needs_wait(g):
                    up_taps(g - 1, 3)
                if s == 1 and needs_wait(g):
                    hidden(g - 1, 1)
                if s == 3 and needs_wait(g):
                    hidden_low(g - 1, 1)
                if s == 4:
                    up_taps(g, 0)
                if s == (16 if first else 8):
                    up_taps(g, 1)
                if s == 20:
                    up_taps(g, 2)
                if s == 21:
                    hidden(g, 0)
                if s == 23:
                    hidden_low(g, 0)

            res_add(7, GC + 7, F0)
            for n in range(2):
                v.memset(up_pad[:, :, n * (S + 1):n * (S + 1) + 1], 0.0).then_inc(ffn_pads, 1)
            dve.wait_ge(ffn_pads, 2)
            for l, s in enumerate(FIRST_SLOTS):
                ffn_slot(0, s, F0 + l)
                if l == 0:
                    h2_low_pair(7)
                if l == 2:
                    invert("COL", 2 * PAIRS + 3, rms_col, 4)
            with dve.Fori(1, GROUPS - 1) as g:
                for s in range(F_SLOTS):
                    ffn_slot(g, s, F_SLOTS * g + (F1 - F_SLOTS + s))
            for l, s in enumerate(FIRST_SLOTS):
                ffn_slot(GROUPS - 1, s, LAST + l)
            for l in range(17):
                if l == 0:
                    up_out(GROUPS - 1, 3, LAST + 16)
                else:
                    res_add((l - 1) % 8, l - 1, LAST + 16 + l)
                if l < 15:
                    split_low(LAST + l + 17, l + 17)
                if l == 0:
                    up_taps(GROUPS - 1, 3)
                if l == 1:
                    hidden(GROUPS - 1, 1)
                if l == 3:
                    hidden_low(GROUPS - 1, 1)

        @block.tensor
        def _(pe):
            mm = nc.tensor.matmul

            def multiply(c, s, dst, high, low, first, last, ready=None, middle=None):
                pe.wait_ge(w_low_ready, c + 1)
                for j in range(KC):
                    if ready is not None:
                        ready(j)
                    if middle is not None and j == KC // 2:
                        middle()
                    for t in range(2):
                        at = NC * j + P * t
                        wh, wl = w_high[:, s % 2, at:at + P], w_low[:, s % 2, at:at + P]
                        mm(dst[:, t, :], wh, high(j), start=first and j == 0, stop=False)
                        mm(dst[:, t, :], wh, low(j), start=False, stop=False)
                        done = mm(dst[:, t, :], wl, high(j), start=False, stop=last and j == KC - 1)
                done.then_inc(chunk_done, 1)

            def h_tiles(tile0):
                return (lambda j: h_high[:, tile0 + j, :]), (lambda j: h_low[:, tile0 + j, :])

            def next_turn(i, name):
                if not (i == 0 and name == "XCOL" if isinstance(i, int) else False):
                    pe.wait_ge(turn_read, t_use(i, name) - 1)

            def token_sums(tiles, col):
                for t in range(QT):
                    for n, tile in enumerate(tiles):
                        last = mm(turn[:, t:t + 1], tile[:, P * t:P * (t + 1)], const_col(col), start=n == 0,
                                  stop=n == len(tiles) - 1)
                last.then_inc(turn_made, 1)

            def head_sums():
                for hh in range(2):
                    for t in range(QT):
                        last = mm(turn[:, QT * hh + t:QT * hh + t + 1], squares[:, hh, P * t:P * (t + 1)],
                                  const_col(K_MEAN_H), start=True, stop=True)
                last.then_inc(turn_made, 1)

            def spread_cols(bank, cols):
                for t in range(QT):
                    last = mm(bank[:, P * t:P * (t + 1)], cols[:, t:t + 1].broadcast_to([P, P]), ident,
                              start=True, stop=True)
                return last

            def attention_slot(i, j, s):
                if s == 1:
                    pe.wait_ge(k_ready, 2 * j + 2)
                    pe.wait_ge(emptied, 5 * j + 5)
                if s in (1, 2):
                    next_turn(i, f"V{s - 1}")
                    for t in range(QT):
                        last = nc.tensor.transpose(turn[:, P * t:P * (t + 1)],
                                                   mixed[:, DT - 3 + s, P * t:P * (t + 1)], ident)
                    last.then_inc(turn_made, 1)
                if 4 <= s <= 11:
                    u = s - 4
                    pe.wait_ge(turn_read, t_use(i, f"P{u}"))
                    if u == 4:
                        pe.wait_ge(o_read, 2 * j + 1)
                    hh, q0 = u // 4, P * (u % 4)
                    for t in range(QT):
                        last = mm(attn_o[:, q0:q0 + P], v_n[:, hh, P * t:P * (t + 1)],
                                  probs_t[:, u % 2, P * t:P * (t + 1)], start=t == 0, stop=t == QT - 1)
                    last.then_inc(pv_done, 1)
                if 3 <= s <= 10:
                    u = s - 3
                    next_turn(i, f"P{u}")
                    pe.wait_ge(probs_ready, 8 * j + (u + 1))
                    for t in range(QT):
                        last = nc.tensor.transpose(turn[:, P * t:P * (t + 1)], probs[:, u % 2, P * t:P * (t + 1)], ident)
                    last.then_inc(turn_made, 1)
                if 1 <= s <= 8:
                    u = s - 1
                    if u >= 2:
                        pe.wait_ge(score_read, 8 * j + (u - 1))
                    hh, q0 = u // 4, P * (u % 4)
                    mm(score[:, u % 2, :], q_t[:, hh, q0:q0 + P], k_t[:, hh, :], start=True, stop=True
                       ).then_inc(score_made, 1)

            def iteration(i):
                first = isinstance(i, int)
                c0 = I_SLOTS * i
                for s in range(I_SLOTS):
                    if first and s == 4:
                        pe.wait_ge(const_in, 16)
                    if first and s == 5:
                        pe.wait_ge(squares_added, 8)
                        token_sums([square_sum[:, 0, :], square_sum[:, 1, :]], K_MEAN_D)
                    if first and s == 6:
                        pe.wait_ge(inverse_ready, 1)
                        spread_cols(turn, rms_col).then_inc(turn_made, 1)
                    if not first:
                        attention_slot(i, i - 1, s)
                    if s == 14:
                        next_turn(i, "Q")
                        pe.wait_ge(head_squares, 2 * i + 1)
                        head_sums()
                    if s == 17:
                        next_turn(i, "K")
                        pe.wait_ge(head_squares, 2 * i + 2)
                        head_sums()
                    if s == 19:
                        pe.wait_ge(inverse_ready, 2 * i + 3)
                        if not first:
                            pe.wait_ge(o_read, 2 * i)
                        spread_cols(turn, rk_col[:, 0:QT])
                        spread_cols(attn_o, rk_col[:, QT:2 * QT]).then_inc(k_spread, 1)
                    y = s // 4
                    if s % 4 == 0 and y in (2, 3):
                        pe.wait_ge(emptied, 5 * i + (y - 1))
                    if s % 4 == 0 and y in (0, 1) and not first:
                        pe.wait_ge(emptied, 5 * i + (y - 2))
                    if s % 4 == 0 and y == 4 and not first:
                        pe.wait_ge(score_read, 8 * i)
                    dst = score if y == 4 else acc[:, 2 * (y % 2):2 * (y % 2) + 2, :]
                    tile0 = KC * (s % 4)
                    ready = None
                    if first and s < 4:
                        def ready(j, tile0=tile0):
                            pe.wait_ge(x_low_ready, tile0 + j + 1)
                    multiply(c0 + s, s, dst, *h_tiles(tile0), s % 4 == 0, s % 4 == 3, ready)

            iteration(0)
            with pe.Fori(1, PAIRS) as i:
                iteration(i)

            def layer_norm_mean():
                next_turn("A", "MU")
                pe.wait_ge(conv_added, CT)
                mm(turn[:], const_col(K_MEAN_C).broadcast_to([P, P]), conv_sum, start=True, stop=True
                   ).then_inc(turn_made, 1)

            def layer_norm_variance():
                next_turn("A", "VAR")
                pe.wait_ge(centred_added, 3)
                token_sums([square_sum[:, 0, :], square_sum[:, 1, :]], K_MEAN_C)

            def layer_norm_row():
                next_turn("A", "ROW")
                pe.wait_ge(inverse_ready, 2 * PAIRS + 2)
                spread_cols(turn, rms_col).then_inc(turn_made, 1)

            def acc_of(group):
                pe.wait_ge(emptied, group - 1)
                return acc[:, 2 * (group % 2):2 * (group % 2) + 2, :]

            pe.wait_ge(mix_low_ready, 2)
            for s in range(8):
                multiply(A0 + s, s, acc_of(GA + s), lambda j: early_high[:, j, :], lambda j: early_low[:, j, :],
                         True, True, middle={2: layer_norm_mean, 5: layer_norm_variance, 6: layer_norm_row}.get(s))

            for s in range(16):
                attention_slot("B", PAIRS - 1, s)
                ready = None
                if s < 2:
                    def ready(j, tile0=KC * s):
                        if j % 2 == 0:
                            pe.wait_ge(mix_low_ready, 3 + (tile0 + j) // 2)
                multiply(B0 + s, s, acc_of(GB + s // 2), *h_tiles(KC * (s % 2)), s % 2 == 0, s % 2 == 1, ready)

            pe.wait_ge(mix_low_ready, 8)
            for n in range(8):
                multiply(C0 + n, n, acc_of(GC + n), *h_tiles(3 * KC), True, True)

            def up_slot(g, s, c):
                if s % 4 == 0:
                    pe.wait_ge(emptied, up_group(g, s // 4) - 1)
                tile0, pair = KC * (s % 4), (s // 4) % 2
                ready = None
                if not needs_wait(g) and s < 4:
                    def ready(j, tile0=tile0):
                        pe.wait_ge(h2_low_ready, tile0 + j + 1)
                multiply(c, s, acc[:, 2 * pair:2 * pair + 2, :], lambda j: h2_high[:, tile0 + j, :],
                         lambda j: h2_low[:, tile0 + j, :], s % 4 == 0, s % 4 == 3, ready)

            def down_slot(g, n, c):
                if n == 0:
                    pe.wait_ge(hid_low_ready, 2 * g + 2)
                pe.wait_ge(emptied, down_group(g, n) - 1)
                high, low = (last_high, last_low) if is_last(g) else (hid_high, hid_low)
                multiply(c, n, acc[:, 2 * (n % 2):2 * (n % 2) + 2, :], lambda j: high[:, j, :],
                         lambda j: low[:, j, :], True, True)

            for s in range(16):
                if s == 2:
                    next_turn("F", "COL")
                    pe.wait_ge(res_squares_added, 8)
                    token_sums([square_sum[:, 0, :], square_sum[:, 1, :]], K_MEAN_D)
                if s == 3:
                    next_turn("F", "ROW")
                    pe.wait_ge(inverse_ready, 2 * PAIRS + 3)
                    spread_cols(turn, rms_col).then_inc(turn_made, 1)
                up_slot(0, s, F0 + s)
            with pe.Fori(1, GROUPS - 1) as g:
                c = F_SLOTS * g + (F1 - F_SLOTS)
                for s in range(8):
                    up_slot(g, s, c + s)
                for n in range(8):
                    down_slot(g - 1, n, c + (8 + n))
                for s in range(8, 16):
                    up_slot(g, s, c + (8 + s))
            for s in range(16):
                up_slot(GROUPS - 1, s, LAST + s)
            for n in range(8):
                down_slot(GROUPS - 2, n, LAST + 16 + n)
            for n in range(8):
                down_slot(GROUPS - 1, n, LAST + 24 + n)


def is_last(g):
    return isinstance(g, int) and g == GROUPS - 1


def needs_wait(i):
    return not (isinstance(i, int) and i == 0)


def constant_table():
    con = np.zeros((P, K_ALL), np.float32)
    con[:, K_ID:K_ID + P] = np.eye(P)
    offset = np.arange(BIAS_W)[None, :] - (S - P) - np.arange(P)[:, None]
    count = sum(((np.abs(offset) <= w // 2) & (offset % d == 0)).astype(int) for w, d in PATTERNS)
    con[:, K_DIST:K_DIST + BIAS_W] = np.abs(offset)
    con[:, K_LOGN:K_LOGN + BIAS_W] = np.where(count > 0, np.log(np.maximum(count, 1)), -1e30)
    con[:, K_MEAN_D] = 1 / D
    con[:, K_MEAN_C] = 1 / (CT * P)
    con[:, K_MEAN_H] = 1 / P
    con[:, K_EPS_R] = 1e-6
    con[:, K_EPS_L] = 1e-5
    con[:, K_SLOPE:K_SLOPE + HEADS] = [-2.0 ** (-8.0 * (h + 1) / HEADS) for h in range(HEADS)]
    return con


def channel_major(a):
    a = np.ascontiguousarray(a)
    a = a.reshape(1, -1) if a.ndim == 1 else a
    k, n = a.shape
    return a.reshape(k, n // P, P).transpose(2, 1, 0).reshape(P, -1)


def kernel(x, norm1_g, w_in, conv_dw_w, conv_dw_b, conv_ln_g, conv_ln_b, q_norm_g, k_norm_g, w_out, norm2_g,
           w_up, ffn_dw_w, ffn_dw_b, w_down):
    import concourse.bacc as bacc
    from concourse.bass_utils import run_bass_kernel_spmd

    params = np.concatenate([channel_major(a) for a in (
        norm1_g, norm2_g, conv_dw_w, conv_dw_b, conv_ln_g, conv_ln_b, q_norm_g, k_norm_g, ffn_dw_w, ffn_dw_b)], axis=1)
    arrays = {
        "x_t": np.ascontiguousarray(np.asarray(x)[0].T.reshape(DT, P, S).transpose(1, 0, 2)),
        "w_in": np.ascontiguousarray(w_in),
        "w_out": np.ascontiguousarray(w_out),
        "w_up": np.ascontiguousarray(w_up),
        "w_down": np.ascontiguousarray(w_down),
        "params": np.ascontiguousarray(params),
        "consts": constant_table(),
    }
    nc = bacc.Bacc("TRN2", target_bir_lowering=False, num_devices=1, dynamic_dma_scratch_size=1024)
    args = [nc.dram_tensor(f"{n}_dram", a.shape, F32, kind="ExternalInput").ap() for n, a in arrays.items()]
    out = nc.dram_tensor("out_dram", (P, DT, S), F32, kind="ExternalOutput").ap()
    hybrid_encoder_layer(nc, *args, out)
    result = run_bass_kernel_spmd(nc, [{f"{n}_dram": a for n, a in arrays.items()}], core_ids=[0])
    y = result.results[0]["out_dram"]
    return np.ascontiguousarray(y.transpose(1, 0, 2).reshape(D, S).T)[None]
```

```python
from contextlib import ExitStack

import numpy as np

import concourse.bass as bass
from concourse import mybir

ALU = mybir.AluOpType
ACT = mybir.ActivationFunctionType
F32 = mybir.dt.float32
F32R = mybir.dt.float32r
FLOAT_MAX = 3.0e38

P = 128
S = 512
QT = S // P
D = 2048
DT = D // P
CT = DT // 2
HEADS = 8
TAPS = 31
PAD = TAPS // 2
F = 5632
FT = F // P
KC = 4
NC = 2 * P
PAIRS = CT // 2
GROUPS = FT // KC
PATTERNS = ((128, 1), (512, 4), (2048, 16))

I_SLOTS = 20
A0 = I_SLOTS * PAIRS
B0 = A0 + D // NC
C0 = B0 + 2 * (D // NC)
F0 = C0 + D // NC
F1 = F0 + 16
F_SLOTS = 24
LAST = F1 + F_SLOTS * (GROUPS - 2)
SLOTS = LAST + F_SLOTS + 8

GA = 5 * PAIRS
GB = GA + D // NC
GC = GB + D // NC
GF = GC + D // NC

C_G1 = 0
C_G2 = C_G1 + DT
C_CW = C_G2 + DT
C_CB = C_CW + CT * TAPS
C_LG = C_CB + CT
C_LB = C_LG + CT
C_QG = C_LB + CT
C_KG = C_QG + 1
C_FW = C_KG + 1
C_FB = C_FW + 2 * FT * 3
C_ALL = C_FB + 2 * FT

BIAS_W = 2 * S - P
K_ID = 0
K_DIST = K_ID + P
K_LOGN = K_DIST + BIAS_W
K_MEAN_D = K_LOGN + BIAS_W
K_MEAN_C = K_MEAN_D + 1
K_MEAN_H = K_MEAN_C + 1
K_EPS_R = K_MEAN_H + 1
K_EPS_L = K_EPS_R + 1
K_SLOPE = K_EPS_L + 1
K_ALL = K_SLOPE + HEADS

T_FIRST = ["XCOL", "XROW", "Q", "K"]
T_PAIR = ["V0", "V1"] + [f"P{u}" for u in range(8)] + ["Q", "K"]
T_NORM = ["MU", "VAR", "ROW"]
T_LAST = T_PAIR[:10]
T_FFN = ["COL", "ROW"]


def t_use(i, name):
    if isinstance(i, str):
        uses = {"A": T_NORM, "B": T_LAST, "F": T_FFN}
        before = len(T_FIRST) + (PAIRS - 1) * len(T_PAIR) + sum(len(uses[k]) for k in uses if k < i)
        return before + uses[i].index(name) + 1
    if isinstance(i, int) and i == 0:
        return T_FIRST.index(name) + 1
    return len(T_PAIR) * i + (len(T_FIRST) - len(T_PAIR) + T_PAIR.index(name) + 1)


SQUARES_IN = {1: (0,), 2: (1,), 3: (2, 3), 4: (4, 5), 5: (6, 7)}


def taps_of(slot):
    count = {9: 4, 10: 6, 11: 6, 12: 3, 13: 6, 14: 6, 15: 6, 16: 3, 17: 5, 18: 5, 19: 2}
    late = {1: 1, 2: 2, 3: 3, 6: 2, 7: 2}
    at = 0
    for s in sorted(count):
        if s == slot:
            return range(at, at + count[s])
        at += count[s]
    for s in sorted(late):
        if s == slot:
            return range(at, at + late[s])
        at += late[s]
    assert at == 2 * TAPS
    return range(0)


def hybrid_encoder_layer(nc, x_t, w_in, w_out, w_up, w_down, params, consts, out):
    with ExitStack() as ctx:
        def sem(name):
            return ctx.enter_context(nc.semaphore(name))

        start = -(-nc.sbuf_base // 32) * 32

        def place(name, shape, dt, offset):
            size = 4 * int(np.prod(shape[1:]))
            assert offset % 32 == 0 and start + offset + size <= nc.sbuf_usable_end, name
            return nc.alloc_sbuf_tensor_at(name, shape, dt, offset=start + offset), -(-(offset + size) // 32) * 32

        par, o = place("channel_params", [P, C_ALL], F32, 0)
        con, o = place("constants", [P, K_ALL], F32, o)
        qk_gain, o = place("qk_gain", [P, 1], F32, o)
        mean_sq, o = place("mean_sq", [P, 8], F32, o)
        std_col, o = place("std_col", [P, 8], F32, o)
        wait_cell, o = place("wait_cell", [P, 1], F32, o)
        table_cell, o = place("table_cell", [P, 1], F32, o)
        newton, o = place("newton", [P, 8], F32, o)
        rms_col, o = place("rms_col", [P, 4], F32, o)
        rq_col, o = place("rq_col", [P, 8], F32, o)
        rk_col, o = place("rk_col", [P, 8], F32, o)
        neg_max, o = place("neg_max", [P, 2], F32, o)
        row_sum, o = place("row_sum", [P, 2], F32, o)
        row_inv, o = place("row_inv", [P, 2], F32, o)
        rms_row, o = place("rms_row", [P, S], F32, o)
        w_raw, o = place("w_raw", [P, 4, KC * NC], F32, o)
        w_high, o = place("w_high", [P, 2, KC * NC], F32R, o)
        w_low, o = place("w_low", [P, 2, KC * NC], F32R, o)
        probs_t_low, _ = place("probs_t_low", [P, QT, 2 * P], F32R, o)
        squares, o = place("squares", [P, 2, S], F32, o)
        ln_mean, ln_rstd = squares[:, 0, :], squares[:, 1, :]
        square_sum, o = place("square_sum", [P, 2, S], F32, o)
        conv_sum = square_sum[:, 0, :]
        res, o = place("residual", [P, DT, S], F32, o)
        r1 = o
        h_high, o = place("h_high", [P, DT, S], F32R, r1)
        h_low, o = place("h_low", [P, DT, S], F32R, o)
        centred_sq, _ = place("centred_sq", [P, CT, S], F32, r1)
        hid_high, f = place("hid_high", [P, KC, S], F32R, r1)
        hid_low, f = place("hid_low", [P, KC, S], F32R, f)
        last_high, f = place("last_high", [P, KC, S], F32R, f)
        last_low, f = place("last_low", [P, KC, S], F32R, f)
        gated, f = place("gated", [P, KC, S], F32, f)
        up_pad, f = place("up_pad", [P, 2, S + 2], F32, f)
        up_conv, f = place("up_conv", [P, 2, S], F32, f)
        assert f <= o
        r2 = o
        mixed, o = place("mixed", [P, DT, S], F32, r2)
        q_low, _ = place("q_low", [P, 2, S], F32R, o)
        q_t, o = place("q_t", [P, 2, S], F32, o)
        k_low, _ = place("k_low", [P, 2, S], F32R, o)
        k_t, o = place("k_t", [P, 2, S], F32, o)
        early_high, e = place("early_high", [P, KC, S], F32R, o)
        early_low, e = place("early_low", [P, KC, S], F32R, e)
        v_high, o = place("v_high", [P, 2, S], F32R, o)
        probs, o = place("probs", [P, 2, S], F32, o)
        probs_t_high, o = place("probs_t_high", [P, QT, 2 * P], F32R, o)
        q_high, o = place("q_high", [P, 2, S], F32R, o)
        assert o == e
        k_high, o = place("k_high", [P, 2, S], F32R, o)
        v_low, o = place("v_low", [P, 2, S], F32R, o)
        bias, o = place("bias", [P, BIAS_W], F32, o)
        glu, o = place("glu", [P, 2, S + 2 * PAD], F32, o)
        h2_high, g = place("h2_high", [P, DT, S], F32R, r2)
        h2_low, g = place("h2_low", [P, DT, S], F32R, g)

        acc = ctx.enter_context(nc.psum_tensor("acc", [P, 4, S], F32))
        score = ctx.enter_context(nc.psum_tensor("score", [P, 2, S], F32))
        turn = ctx.enter_context(nc.psum_tensor("turn", [P, S], F32))
        attn_o = ctx.enter_context(nc.psum_tensor("attn_o", [P, S], F32))

        ident = con[:, K_ID:K_ID + P]

        turn_tiles = turn[:].rearrange("p (t n) -> p t n", n=P)

        def const_col(c):
            return con[:, c:c + 1]

        def param(c):
            return par[:, bass.ds(c, 1)]

        gain_in, params_in, const_in = sem("gain_in"), sem("params_in"), sem("const_in")
        x_in = [sem(f"x_in{k}") for k in range(4)]
        w_arrived = [sem(f"w_arrived{k}") for k in range(4)]
        w_high_ready, w_low_ready, chunk_done = sem("w_high_ready"), sem("w_low_ready"), sem("chunk_done")
        x_high_ready, x_low_ready = sem("x_high_ready"), sem("x_low_ready")
        squares_ready, squares_added = sem("squares_ready"), sem("squares_added")
        emptied = sem("emptied")
        turn_made, turn_high, turn_read = sem("turn_made"), sem("turn_high"), sem("turn_read")
        x0_in = [sem(f"x0_in{j}") for j in range(KC)]
        w0_in = [sem(f"w0_in{j}") for j in range(KC - 1)]
        w0_high, w0_low, table_loaded = sem("w0_high"), sem("w0_low"), sem("table_loaded")
        std_ready, newton_step = sem("std_ready"), sem("newton_step")
        inverse_ready, gain_ready, pads_ready, sum_cleared = (sem(n) for n in (
            "inverse_ready", "gain_ready", "pads_ready", "sum_cleared"))
        sigmoid_ready, glu_ready, tap_done, conv_added = (sem(n) for n in (
            "sigmoid_ready", "glu_ready", "tap_done", "conv_added"))
        head_squares, k_spread, k_ready = sem("head_squares"), sem("k_spread"), sem("k_ready")
        qk_high_ready, qk_low_ready = sem("qk_high_ready"), sem("qk_low_ready")
        bias_ready, score_made, score_read, max_ready, exp_done, sum_inverted, probs_ready, pv_done, o_read = (
            sem(n) for n in ("bias_ready", "score_made", "score_read", "max_ready", "exp_done",
                             "sum_inverted", "probs_ready", "pv_done", "o_read"))
        centred, centred_squares, centred_added, scaled, conv_out = (sem(n) for n in (
            "centred", "centred_squares", "centred_added", "scaled", "conv_out"))
        mix_high_ready, mix_low_ready = sem("mix_high_ready"), sem("mix_low_ready")
        h2_high_ready, h2_low_ready, res_squares, res_squares_added = (sem(n) for n in (
            "h2_high_ready", "h2_low_ready", "res_squares", "res_squares_added"))
        ffn_pads, up_mid, up_side, gate_act, hidden_ready, hid_high_ready, hid_low_ready = (sem(n) for n in (
            "ffn_pads", "up_mid", "up_side", "gate_act", "hidden_ready", "hid_high_ready", "hid_low_ready"))
        out_written = sem("out_written")

        def weight_slab(w, tile0, col):
            rows = w.rearrange("(t p) n -> p t n", p=P)
            return rows[:, bass.ds(tile0, KC), bass.ds(col, NC)]

        def in_slab(i, s):
            return weight_slab(w_in, KC * (s % 4), 4 * NC * (s // 4) + NC * i)

        def ffn_slab(g, s):
            if s < 8:
                return weight_slab(w_up, KC * (s % 4), KC * P * g + NC * (s // 4))
            if s < 16:
                return weight_slab(w_down, KC * (g - 1), NC * (s - 8))
            return weight_slab(w_up, KC * (s % 4), KC * P * g + (F + NC * ((s - 16) // 4)))

        FIRST_SLOTS = [*range(8), *range(16, F_SLOTS)]

        def up_group(g, y):
            if isinstance(g, int) and g in (0, GROUPS - 1):
                return (GF if g == 0 else 12 * (GROUPS - 2) + GF + 4) + y
            return 12 * g + (GF - 8 + (y if y < 2 else y + 8))

        def down_group(g, n):
            if isinstance(g, int) and g >= GROUPS - 2:
                return 12 * (GROUPS - 2) + (GF + 8 + 8 * (g - GROUPS + 2) + n)
            return 12 * g + (GF + 6 + n)

        block = ctx.enter_context(nc.Block())

        @block.sync
        def _(sp):
            def fetch(c, s, slab, wait=True):
                if wait:
                    sp.wait_ge(w_low_ready, c - 3)
                sp.dma_start(w_raw[:, s % 4, :].rearrange("p (t n) -> p t n", n=NC), slab).then_inc(
                    w_arrived[s % 4], 16)

            sp.dma_start(par[:, 0:C_G2], params[:, 0:C_G2]).then_inc(gain_in, 16)
            for j in range(KC):
                sp.dma_start(res[:, j, :], x_t[:, j, :]).then_inc(x0_in[j], 16)
                sp.dma_start(w_raw[:, 0, NC * j:NC * (j + 1)], w_in[P * j:P * (j + 1), 0:NC]).then_inc(
                    w_arrived[0] if j == KC - 1 else w0_in[j], 16)
            for k in range(1, 4):
                fetch(k, k, in_slab(0, k), wait=False)
                sp.dma_start(res[:, KC * k:KC * (k + 1), :], x_t[:, KC * k:KC * (k + 1), :]).then_inc(x_in[k], 16)
            sp.dma_start(con[:], consts).then_inc(const_in, 16)
            sp.dma_start(par[:, C_G2:], params[:, C_G2:]).then_inc(params_in, 16)
            for s in range(4, I_SLOTS):
                fetch(s, s, in_slab(0, s))
            with sp.Fori(1, PAIRS) as i:
                for s in range(I_SLOTS):
                    fetch(I_SLOTS * i + s, s, in_slab(i, s))
            for n in range(8):
                fetch(A0 + n, A0 + n, weight_slab(w_out, 2 * KC, NC * n))
            for n in range(8):
                for b in range(2):
                    fetch(B0 + 2 * n + b, 2 * n + b, weight_slab(w_out, KC * b, NC * n))
            for n in range(8):
                fetch(C0 + n, n, weight_slab(w_out, 3 * KC, NC * n))
            for l, s in enumerate(FIRST_SLOTS):
                fetch(F0 + l, l, ffn_slab(0, s))
            with sp.Fori(1, GROUPS - 1) as g:
                for s in range(F_SLOTS):
                    fetch(F_SLOTS * g + (F1 - F_SLOTS + s), s, ffn_slab(g, s))
            for l, s in enumerate(FIRST_SLOTS):
                fetch(LAST + l, l, ffn_slab(GROUPS - 1, s))
            for l in range(16):
                fetch(LAST + 16 + l, l, ffn_slab(GROUPS - 1 + l // 8, 8 + l % 8))
            for n in range(7):
                sp.wait_ge(emptied, down_group(GROUPS - 1, n) + 1)
                sp.dma_start(out[:, 2 * n:2 * n + 2, :], res[:, 2 * n:2 * n + 2, :]).then_inc(out_written, 16)
            for t in range(2):
                sp.wait_ge(emptied, down_group(GROUPS - 1, 7) + t + 1)
                sp.dma_start(out[:, DT - 2 + t, :], res[:, DT - 2 + t, :]).then_inc(out_written, 16)
            sp.wait_ge(out_written, 16 * 9)

        @block.gpsimd
        def _(pool):
            pool.wait_ge(turn_made, t_use(0, "XCOL"))
            nc.gpsimd.memset(conv_sum, 0.0).then_inc(sum_cleared, 1)

            def add_tile(i, t):
                first = isinstance(i, int) and t == 0
                if first:
                    pool.wait_ge(sum_cleared, 1)
                else:
                    pool.wait_ge(conv_added, 2 * i + t)
                if t == 0:
                    pool.wait_ge(tap_done, 2 * TAPS * i + 2 * TAPS)
                nc.gpsimd.tensor_tensor(conv_sum.rearrange("p (o n) -> p o n", o=1),
                                        conv_sum.rearrange("p (o n) -> p o n", o=1),
                                        mixed[:, bass.ds(2 * i + t, 1), :], ALU.add).then_inc(conv_added, 1)

            add_tile(0, 0)
            add_tile(0, 1)
            with pool.Fori(1, PAIRS - 1) as i:
                add_tile(i, 0)
                add_tile(i, 1)

        @block.scalar
        def _(act):
            def split_high(c, s, buffer_used=True):
                act.wait_ge(w_arrived[s % 4], 4 * (c - s % 4) + 16)
                if buffer_used:
                    act.wait_ge(chunk_done, c - 1)
                nc.scalar.activation(w_high[:, s % 2, :], w_raw[:, s % 4, :], ACT.Copy).then_inc(w_high_ready, 1)

            def x_chunk(k):
                if k:
                    act.wait_ge(x_in[k], 16)
                for j in range(KC * k, KC * (k + 1)):
                    if k == 0:
                        act.wait_ge(x0_in[j], 16)
                    nc.scalar.activation(h_high[:, j, :], res[:, j, :], ACT.Copy, scale=param(C_G1 + j)
                                         ).then_inc(x_high_ready, 1)
                    if k == 0:
                        act.wait_ge(w_arrived[0] if j == KC - 1 else w0_in[j], 16)
                        nc.scalar.activation(w_high[:, 0, NC * j:NC * (j + 1)], w_raw[:, 0, NC * j:NC * (j + 1)],
                                             ACT.Copy).then_inc(w_high_ready if j == KC - 1 else w0_high, 1)
                if k == 0:
                    split_high(1, 1, buffer_used=False)

            def x_squares(n):
                if n:
                    act.wait_ge(squares_added, n)
                nc.scalar.activation(squares[:], res[:, 2 * n:2 * n + 2, :], ACT.Square).then_inc(squares_ready, 1)

            def turn_copy(i, name, dst):
                act.wait_ge(turn_made, t_use(i, name))
                nc.scalar.activation(dst, turn[:], ACT.Copy).then_inc(turn_read, 1)

            def turn_high_part(i, name, dst, bank):
                act.wait_ge(turn_made, t_use(i, name))
                nc.scalar.activation(dst, bank, ACT.Copy).then_inc(turn_high, 1)

            def turn_sqrt(i, name, n, width, eps):
                act.wait_ge(turn_made, t_use(i, name))
                nc.scalar.activation(mean_sq[:, 0:width], turn[:, 0:width], ACT.Identity, bias=const_col(eps)
                                     ).then_inc(turn_read, 1)
                act.wait_ge(turn_read, t_use(i, name))
                nc.scalar.activation(std_col[:, 0:width], mean_sq[:, 0:width], ACT.Sqrt).then_inc(std_ready, 1)

            def scale_unit(i, j, u):
                act.wait_ge(score_made, 8 * j + (u + 1))
                if u >= 2:
                    act.wait_ge(turn_made, t_use(i, f"P{u - 2}"))
                nc.scalar.activation(probs[:, u % 2, :], score[:, u % 2, :], ACT.Copy, scale=rq_col[:, u:u + 1]
                                     ).then_inc(score_read, 1)

            def exp_unit(j, u):
                act.wait_ge(max_ready, 8 * j + (u + 1))
                nc.scalar.activation(probs[:, u % 2, :], probs[:, u % 2, :], ACT.Exp, bias=neg_max[:, u % 2:u % 2 + 1],
                                     scale=-1.0, accum_out=row_sum[:, u % 2:u % 2 + 1]).then_inc(exp_done, 1)

            def normalise_unit(j, u):
                act.wait_ge(sum_inverted, 8 * j + (u + 1))
                nc.scalar.activation(probs[:, u % 2, :], probs[:, u % 2, :], ACT.Copy,
                                     scale=row_inv[:, u % 2:u % 2 + 1]).then_inc(probs_ready, 1)

            def k_split_high(j):
                act.wait_ge(k_ready, 2 * j + 2)
                nc.scalar.activation(k_high[:], k_t[:], ACT.Copy).then_inc(qk_high_ready, 1)

            def q_split_high():
                nc.scalar.activation(q_high[:], q_t[:], ACT.Copy).then_inc(qk_high_ready, 1)

            def attention_slot(i, j, s):
                if s == 0 and not isinstance(i, str):
                    k_split_high(j)
                    q_split_high()
                if s in (1, 2):
                    turn_high_part(i, f"V{s - 1}", v_high[:, s - 1, :], turn[:])
                if 3 <= s <= 10:
                    u = s - 3
                    if u >= 2 and u % 2 == 0:
                        act.wait_ge(pv_done, 4 * j + u // 2)
                    turn_high_part(i, f"P{u}", probs_t_high[:, :, P * (u % 2):P * (u % 2 + 1)], turn_tiles)
                if s == 1:
                    act.wait_ge(inverse_ready, 2 * j + 2)
                if 1 <= s <= 8:
                    scale_unit(i, j, s - 1)
                if 2 <= s <= 9:
                    normalise_unit(j, s - 2)
                if 1 <= s <= 8:
                    exp_unit(j, s - 1)
                if s in (7, 11):
                    hh = s // 11
                    act.wait_ge(pv_done, 4 * j + (2 * hh + 2))
                    nc.scalar.activation(mixed[:, bass.ds(2 * j + (CT + hh), 1), :], attn_o[:].rearrange(
                        "p (o n) -> p o n", o=1), ACT.Copy).then_inc(o_read, 1)

            def iteration(i):
                first = isinstance(i, int)
                c0 = I_SLOTS * i
                for s in range(I_SLOTS):
                    if not (first and s == 0):
                        split_high(c0 + (s + 1), s + 1)
                    if first and s < 3:
                        x_chunk(s + 1)
                    if first:
                        for n in SQUARES_IN.get(s, ()):
                            x_squares(n)
                    if first and s == 6:
                        turn_sqrt(0, "XCOL", 1, 4, K_EPS_R)
                    if first and s == 7:
                        turn_copy(0, "XROW", rms_row[:])
                    if not first:
                        attention_slot(i, i - 1, s)
                    if s == 8:
                        act.wait_ge(emptied, 5 * i + 2)
                        nc.scalar.activation(q_t[:], q_t[:], ACT.Sigmoid).then_inc(sigmoid_ready, 1)
                    if s == 12:
                        act.wait_ge(emptied, 5 * i + 3)
                        nc.scalar.activation(squares[:], q_t[:], ACT.Square).then_inc(head_squares, 1)
                    if s == 14:
                        turn_sqrt(i, "Q", 2 * i + 2, 8, K_EPS_R)
                    if s == 16:
                        act.wait_ge(emptied, 5 * i + 4)
                        act.wait_ge(turn_made, t_use(i, "Q"))
                        nc.scalar.activation(squares[:], k_t[:], ACT.Square).then_inc(head_squares, 1)
                    if s == 17:
                        act.wait_ge(inverse_ready, 2 * i + 2)
                        turn_sqrt(i, "K", 2 * i + 3, 8, K_EPS_R)

            def mix_high(pair):
                nc.scalar.activation(h_high[:, 2 * pair:2 * pair + 2, :], mixed[:, 2 * pair:2 * pair + 2, :],
                                     ACT.Copy).then_inc(mix_high_ready, 1)

            act.wait_ge(pads_ready, 1)
            nc.scalar.activation(table_cell[:], glu[:, 0, 0:1], ACT.Copy).then_inc(table_loaded, 1)
            act.wait_ge(gain_in, 16)
            x_chunk(0)
            iteration(0)
            act.wait_ge(params_in, 16)
            with act.Fori(1, PAIRS) as i:
                iteration(i)

            act.wait_ge(o_read, 6)
            for n in range(2):
                nc.scalar.activation(early_high[:, 2 * n:2 * n + 2, :], mixed[:, CT + 2 * n:CT + 2 * n + 2, :],
                                     ACT.Copy).then_inc(mix_high_ready, 1)

            for s in range(8):
                if s < 7:
                    split_high(A0 + s + 1, s + 1)
                if s == 2:
                    turn_copy("A", "MU", ln_mean)
                if s == 3:
                    act.wait_ge(chunk_done, A0)
                    for n in range(4):
                        act.wait_ge(centred, n + 1)
                        nc.scalar.activation(centred_sq[:, 2 * n:2 * n + 2, :], mixed[:, 2 * n:2 * n + 2, :],
                                             ACT.Square).then_inc(centred_squares, 1)
                if s == 5:
                    turn_sqrt("A", "VAR", 2 * PAIRS + 2, 4, K_EPS_L)
                    act.wait_ge(table_loaded, 1)
                    nc.scalar.activation(table_cell[:], table_cell[:], ACT.Silu).then_inc(table_loaded, 1)
                    k_split_high(PAIRS - 1)
                if s == 6:
                    turn_copy("A", "ROW", ln_rstd)
                    for n in range(4):
                        act.wait_ge(scaled, n + 1)
                        for j in (2 * n, 2 * n + 1):
                            nc.scalar.activation(mixed[:, j, :], mixed[:, j, :], ACT.Silu, scale=param(C_LG + j),
                                                 bias=param(C_LB + j)).then_inc(conv_out, 1)
                        act.wait_ge(conv_out, 2 * n + 2)
                        mix_high(n)
                        if n == 0:
                            split_high(B0, 0)
                        if n == 2:
                            split_high(B0 + 1, 1)
                            act.wait_ge(chunk_done, B0)
                            q_split_high()

            def h2_high_pair(n):
                act.wait_ge(emptied, GC + n + 1)
                for j in (2 * n, 2 * n + 1):
                    nc.scalar.activation(h2_high[:, j, :], res[:, j, :], ACT.Copy, scale=param(C_G2 + j)
                                         ).then_inc(h2_high_ready, 1)
                if n:
                    act.wait_ge(res_squares_added, n)
                nc.scalar.activation(squares[:], res[:, 2 * n:2 * n + 2, :], ACT.Square).then_inc(res_squares, 1)

            for s in range(16):
                if s:
                    split_high(B0 + s + 1, s + 1)
                attention_slot("B", PAIRS - 1, s)
                if s == 12:
                    act.wait_ge(o_read, HEADS)
                    mix_high(6)
                    mix_high(7)

            for n in range(8):
                split_high(C0 + n + 1, n + 1)
                if n == 1:
                    act.wait_ge(mix_low_ready, 8)
                if n:
                    h2_high_pair(n - 1)

            def up_act(g, y):
                act.wait_ge(emptied, up_group(g, y) + 1)
                if y == 0 and needs_wait(g):
                    act.wait_ge(hidden_ready, 2 * g)
                if y == 3:
                    act.wait_ge(hidden_ready, 2 * g + 1)
                for t in range(2):
                    f = FT * (y // 2) + 2 * (y % 2) + t
                    nc.scalar.activation(up_conv[:, t, :], up_pad[:, t, 1:S + 1], ACT.Identity,
                                         scale=param(3 * KC * g + (C_FW + 3 * f + 1)),
                                         bias=param(KC * g + (C_FB + f))).then_inc(up_mid, 1)

            def gate_swish(g, y):
                act.wait_ge(up_side, 16 * g + (4 * y + 4))
                if needs_wait(g):
                    act.wait_ge(hid_low_ready, 2 * g + (y - 1))
                nc.scalar.activation(gated[:, 2 * y:2 * y + 2, :], up_conv[:], ACT.Silu).then_inc(gate_act, 1)

            def hidden_high(g, y):
                act.wait_ge(hidden_ready, 2 * g + (y + 1))
                high = hid_high
                if is_last(g):
                    high = last_high
                elif y == 0 and needs_wait(g):
                    act.wait_ge(chunk_done, F_SLOTS * g + (F1 - F_SLOTS + 16))
                nc.scalar.activation(high[:, 2 * y:2 * y + 2, :], gated[:, 2 * y:2 * y + 2, :], ACT.Copy
                                     ).then_inc(hid_high_ready, 1)

            def ffn_slot(g, s, c):
                first = isinstance(g, int)
                split_high(c + 1, c + 1 if first else s + 1)
                if s == 0 and needs_wait(g):
                    up_act(g - 1, 3)
                if s == 2 and needs_wait(g):
                    hidden_high(g - 1, 1)
                if s == 4:
                    up_act(g, 0)
                if s == 5:
                    gate_swish(g, 0)
                if s == (16 if first else 8):
                    up_act(g, 1)
                if s == (17 if first else 9):
                    gate_swish(g, 1)
                if s == 20:
                    up_act(g, 2)
                if s == 22:
                    hidden_high(g, 0)

            for l, s in enumerate(FIRST_SLOTS):
                ffn_slot(0, s, F0 + l)
                if l == 0:
                    h2_high_pair(7)
                if l == 2:
                    turn_sqrt("F", "COL", 2 * PAIRS + 3, 4, K_EPS_R)
                if l == 3:
                    turn_copy("F", "ROW", rms_row[:])
            with act.Fori(1, GROUPS - 1) as g:
                for s in range(F_SLOTS):
                    ffn_slot(g, s, F_SLOTS * g + (F1 - F_SLOTS + s))
            for l, s in enumerate(FIRST_SLOTS):
                ffn_slot(GROUPS - 1, s, LAST + l)
            for l in range(16):
                if l < 15:
                    split_high(LAST + l + 17, l + 17)
                if l == 0:
                    up_act(GROUPS - 1, 3)
                if l == 2:
                    hidden_high(GROUPS - 1, 1)

        @block.vector
        def _(dve):
            v = nc.vector

            def split_low(c, s):
                dve.wait_ge(w_high_ready, c + 1)
                v.tensor_tensor(w_low[:, s % 2, :], w_raw[:, s % 4, :], w_high[:, s % 2, :].bitcast(F32),
                                ALU.subtract).then_inc(w_low_ready, 1)

            def add_halves(added, n):
                dve.wait_ge(added, n)
                v.tensor_tensor(square_sum[:, 0, :], square_sum[:, 0, :], square_sum[:, 1, :], ALU.add
                                ).then_inc(added, 1)

            def add_squares(n, ready, added):
                dve.wait_ge(ready, n + 1)
                if n == 0:
                    v.tensor_copy(square_sum[:], squares[:]).then_inc(added, 1)
                else:
                    dve.wait_ge(added, n)
                    v.tensor_tensor(square_sum[:], square_sum[:], squares[:], ALU.add).then_inc(added, 1)
                if n == DT // 2 - 1:
                    add_halves(added, n + 1)

            def x_chunk(k):
                for j in range(KC * k, KC * (k + 1)):
                    dve.wait_ge(x_high_ready, j + 1)
                    v.scalar_tensor_tensor(out=h_low[:, j, :], in0=res[:, j, :], scalar=param(C_G1 + j),
                                           in1=h_high[:, j, :].bitcast(F32), op0=ALU.mult, op1=ALU.subtract
                                           ).then_inc(x_low_ready, 1)
                    if k == 0:
                        at = slice(NC * j, NC * (j + 1))
                        if j == KC - 1:
                            dve.wait_ge(w_high_ready, 1)
                        else:
                            dve.wait_ge(w0_high, j + 1)
                        v.tensor_tensor(w_low[:, 0, at], w_raw[:, 0, at], w_high[:, 0, at].bitcast(F32),
                                        ALU.subtract).then_inc(w_low_ready if j == KC - 1 else w0_low, 1)
                if k == 0:
                    split_low(1, 1)

            def spread(row):
                return row.rearrange("p (o n) -> p o n", o=1).broadcast_to([P, 2, S])

            def scale_out(c_done, src, dst):
                dve.wait_ge(chunk_done, c_done)
                v.tensor_tensor(dst, src, spread(rms_row[:]), ALU.mult).then_inc(emptied, 1)

            def invert(name, n, dst, width):
                r, step, mean = dst[:, 0:width], newton[:, 0:width], mean_sq[:, 0:width]
                dve.wait_ge(std_ready, n)
                v.reciprocal(r, std_col[:, 0:width]).then_inc(newton_step, 1)
                dve.wait_ge(newton_step, 4 * n - 3)
                v.tensor_tensor(step, r, r, ALU.mult).then_inc(newton_step, 1)
                dve.wait_ge(newton_step, 4 * n - 2)
                v.tensor_tensor(step, step, mean, ALU.mult).then_inc(newton_step, 1)
                dve.wait_ge(newton_step, 4 * n - 1)
                v.tensor_scalar(step, step, -0.5, 1.5, ALU.mult, ALU.add).then_inc(newton_step, 1)
                dve.wait_ge(newton_step, 4 * n)
                v.tensor_tensor(r, r, step, ALU.mult).then_inc(inverse_ready, 1)

            def taps(i, steps):
                for m in steps:
                    k, t = m // 2, m % 2
                    y = mixed[:, bass.ds(2 * i + t, 1), :]
                    src = glu[:, t:t + 1, k:k + S]
                    w = param(2 * TAPS * i + (C_CW + TAPS * t + k))
                    if k == 0:
                        v.tensor_scalar(y, src, w, param(2 * i + (C_CB + t)), ALU.mult, ALU.add).then_inc(tap_done, 1)
                    else:
                        dve.wait_ge(tap_done, 2 * TAPS * i + (m - 1))
                        v.scalar_tensor_tensor(out=y, in0=src, scalar=w, in1=y, op0=ALU.mult, op1=ALU.add
                                               ).then_inc(tap_done, 1)

            def bias_table(j, hh):
                v.scalar_tensor_tensor(out=bias[:], in0=con[:, K_DIST:K_DIST + BIAS_W],
                                       scalar=con[:, bass.ds(2 * j + (K_SLOPE + hh), 1)],
                                       in1=con[:, K_LOGN:K_LOGN + BIAS_W], op0=ALU.mult, op1=ALU.add
                                       ).then_inc(bias_ready, 1)

            def score_unit(j, u):
                dve.wait_ge(score_read, 8 * j + (u + 1))
                dve.wait_ge(bias_ready, 2 * j + (u // 4 + 1))
                v.memset(wait_cell[:], 0.0)
                x0 = P * (QT - 1 - u % QT)
                v.tensor_tensor_reduce(probs[:, u % 2, :], probs[:, u % 2, :], bias[:, x0:x0 + S], -1.0, FLOAT_MAX,
                                       ALU.add, ALU.min, neg_max[:, u % 2:u % 2 + 1]).then_inc(max_ready, 1)

            def invert_sum(j, u):
                dve.wait_ge(exp_done, 8 * j + (u + 1))
                v.reciprocal(row_inv[:, u % 2:u % 2 + 1], row_sum[:, u % 2:u % 2 + 1]).then_inc(sum_inverted, 1)

            def k_split_low(j):
                dve.wait_ge(qk_high_ready, 2 * j + 1)
                v.tensor_tensor(k_low[:], k_t[:], k_high[:].bitcast(F32), ALU.subtract).then_inc(qk_low_ready, 1)

            def q_split_low(j):
                dve.wait_ge(qk_high_ready, 2 * j + 2)
                v.tensor_tensor(q_low[:], q_t[:], q_high[:].bitcast(F32), ALU.subtract).then_inc(qk_low_ready, 1)

            def attention_slot(j, s):
                if s == 0 and not isinstance(j, int):
                    k_split_low(j)
                    q_split_low(j)
                if 2 <= s <= 9:
                    invert_sum(j, s - 2)
                if s == 1:
                    bias_table(j, 0)
                if s == 5:
                    bias_table(j, 1)
                if 1 <= s <= 8:
                    score_unit(j, s - 1)
                if 1 <= s <= 10:
                    dve.wait_ge(turn_high, 10 * j + s)
                    if s < 3:
                        v.tensor_tensor(v_low[:, s - 1, :], turn[:], v_high[:, s - 1, :].bitcast(F32), ALU.subtract
                                        ).then_inc(turn_read, 1)
                    else:
                        at = slice(P * ((s - 3) % 2), P * ((s - 3) % 2 + 1))
                        v.tensor_tensor(probs_t_low[:, :, at], turn_tiles, probs_t_high[:, :, at].bitcast(F32),
                                        ALU.subtract).then_inc(turn_read, 1)

            def v_out(i):
                scale_out(I_SLOTS * i + I_SLOTS, score[:], mixed[:, DT - 2:DT, :])

            def iteration(i):
                first = isinstance(i, int)
                c0 = I_SLOTS * i
                for s in range(I_SLOTS):
                    if s == 0 and not first:
                        v_out(i - 1)
                    if s == 4 and not first:
                        scale_out(c0 + 4, acc[:, 0:2, :], mixed[:, bass.ds(2 * i, 2), :])
                    if s == 8:
                        if not first:
                            dve.wait_ge(score_made, 8 * i)
                        scale_out(c0 + 8, acc[:, 2:4, :], q_t[:])
                    if s == 12:
                        scale_out(c0 + 12, acc[:, 0:2, :], q_t[:])
                    if s == 15:
                        invert("Q", 2 * i + 2, rq_col, 8)
                    if s == 16:
                        scale_out(c0 + 16, acc[:, 2:4, :], k_t[:])
                    if s == 18:
                        invert("K", 2 * i + 3, rk_col, 8)
                    if not (first and s == 0):
                        split_low(c0 + (s + 1), s + 1)
                    if first and s < 3:
                        x_chunk(s + 1)
                    if first:
                        for n in SQUARES_IN.get(s, ()):
                            add_squares(n, squares_ready, squares_added)
                    if first and s == 5:
                        dve.wait_ge(params_in, 16)
                        v.scalar_tensor_tensor(out=qk_gain[:], in0=param(C_QG), scalar=float(P) ** -0.5,
                                               in1=param(C_KG), op0=ALU.mult, op1=ALU.mult).then_inc(gain_ready, 1)
                        dve.wait_ge(gain_ready, 1)
                    if first and s == 6:
                        invert("XCOL", 1, rms_col, 4)
                    if not first:
                        attention_slot(i - 1, s)
                        if s < 9:
                            taps(i - 1, taps_of(s))
                    if s == 9:
                        dve.wait_ge(sigmoid_ready, i + 1)
                        if first:
                            dve.wait_ge(pads_ready, 2)
                        v.tensor_tensor(glu[:, :, PAD:PAD + S], mixed[:, bass.ds(2 * i, 2), :], q_t[:], ALU.mult
                                        ).then_inc(glu_ready, 1)
                        dve.wait_ge(glu_ready, i + 1)
                    if s >= 9:
                        taps(i, taps_of(s))
                    if first and s == 7:
                        dve.wait_ge(turn_read, t_use(0, "XROW"))
                        scale_out(4, acc[:, 0:2, :], mixed[:, 0:2, :])
                    if s == 19:
                        dve.wait_ge(k_spread, i + 1)
                        for hh, bank in ((0, turn), (1, attn_o)):
                            v.scalar_tensor_tensor(out=k_t[:, hh, :], in0=k_t[:, hh, :], scalar=qk_gain[:, 0:1],
                                                   in1=bank[:], op0=ALU.mult, op1=ALU.mult).then_inc(k_ready, 1)

            def mix_low(n, pair):
                dve.wait_ge(mix_high_ready, n + 3)
                v.tensor_tensor(h_low[:, 2 * pair:2 * pair + 2, :], mixed[:, 2 * pair:2 * pair + 2, :],
                                h_high[:, 2 * pair:2 * pair + 2, :].bitcast(F32), ALU.subtract
                                ).then_inc(mix_low_ready, 1)

            def res_add(n, group, c_done):
                dve.wait_ge(chunk_done, c_done)
                pair = group % 2 if isinstance(group, int) else n % 2
                v.tensor_tensor(res[:, 2 * n:2 * n + 2, :], res[:, 2 * n:2 * n + 2, :],
                                acc[:, 2 * pair:2 * pair + 2, :], ALU.add).then_inc(emptied, 1)

            v.memset(glu[:, :, 0:PAD], 0.0).then_inc(pads_ready, 1)
            v.memset(glu[:, :, PAD + S:], 0.0).then_inc(pads_ready, 1)
            dve.wait_ge(gain_in, 16)
            x_chunk(0)
            iteration(0)
            dve.wait_ge(const_in, 16)
            with dve.Fori(1, PAIRS) as i:
                iteration(i)

            def centre(n):
                v.tensor_tensor(mixed[:, 2 * n:2 * n + 2, :], mixed[:, 2 * n:2 * n + 2, :], spread(ln_mean),
                                ALU.subtract).then_inc(centred, 1)

            def add_centred(n):
                dve.wait_ge(centred_squares, n + 1)
                if n == 1:
                    v.tensor_tensor(square_sum[:], centred_sq[:, 0:2, :], centred_sq[:, 2:4, :], ALU.add
                                    ).then_inc(centred_added, 1)
                else:
                    dve.wait_ge(centred_added, n - 1)
                    v.tensor_tensor(square_sum[:], square_sum[:], centred_sq[:, 2 * n:2 * n + 2, :], ALU.add
                                    ).then_inc(centred_added, 1)

            def scale_conv(n):
                v.tensor_tensor(mixed[:, 2 * n:2 * n + 2, :], mixed[:, 2 * n:2 * n + 2, :], spread(ln_rstd),
                                ALU.mult).then_inc(scaled, 1)

            for n in range(2):
                dve.wait_ge(mix_high_ready, n + 1)
                v.tensor_tensor(early_low[:, 2 * n:2 * n + 2, :], mixed[:, CT + 2 * n:CT + 2 * n + 2, :],
                                early_high[:, 2 * n:2 * n + 2, :].bitcast(F32), ALU.subtract
                                ).then_inc(mix_low_ready, 1)

            for s in range(8):
                if s == 0:
                    v_out(PAIRS - 1)
                else:
                    res_add(s - 1, GA + s - 1, A0 + s)
                split_low(A0 + s + 1, s + 1)
                if s < 2:
                    for late in ((1, 2, 3), (6, 7))[s]:
                        taps(PAIRS - 1, taps_of(late))
                if s == 1:
                    for t in range(2):
                        dve.wait_ge(tap_done, 2 * TAPS * PAIRS - 1 + t)
                        dve.wait_ge(conv_added, CT - 2 + t)
                        v.tensor_tensor(conv_sum, conv_sum, mixed[:, CT - 2 + t, :], ALU.add).then_inc(conv_added, 1)
                if s == 2:
                    dve.wait_ge(turn_read, t_use("A", "MU"))
                    for n in range(3):
                        centre(n)
                if s == 3:
                    centre(3)
                    add_centred(1)
                    add_centred(2)
                if s == 4:
                    add_centred(3)
                    add_halves(centred_added, 3)
                if s == 5:
                    invert("VAR", 2 * PAIRS + 2, rms_col, 4)
                    k_split_low(PAIRS - 1)
                if s == 6:
                    dve.wait_ge(turn_read, t_use("A", "ROW"))
                    for n in range(3):
                        scale_conv(n)
                    mix_low(0, 0)
                if s == 7:
                    scale_conv(3)
                    mix_low(1, 1)
                    mix_low(2, 2)
                    split_low(B0 + 1, 1)

            def h2_low_pair(n):
                for j in (2 * n, 2 * n + 1):
                    dve.wait_ge(h2_high_ready, j + 1)
                    v.scalar_tensor_tensor(out=h2_low[:, j, :], in0=res[:, j, :], scalar=param(C_G2 + j),
                                           in1=h2_high[:, j, :].bitcast(F32), op0=ALU.mult, op1=ALU.subtract
                                           ).then_inc(h2_low_ready, 1)
                add_squares(n, res_squares, res_squares_added)

            for s in range(16):
                if s and s % 2 == 0:
                    res_add(s // 2 - 1, GB + s // 2 - 1, B0 + s)
                if s == 0:
                    q_split_low(PAIRS - 1)
                    mix_low(3, 3)
                    res_add(7, GA + 7, B0)
                else:
                    split_low(B0 + s + 1, s + 1)
                attention_slot(PAIRS - 1, s)
                if s == 12:
                    mix_low(4, 6)
                    mix_low(5, 7)

            for n in range(8):
                if n == 0:
                    res_add(7, GB + 7, C0)
                else:
                    res_add(n - 1, GC + n - 1, C0 + n)
                split_low(C0 + n + 1, n + 1)
                if n:
                    h2_low_pair(n - 1)

            def up_out(g, y, c_done):
                if y or needs_wait(g):
                    dve.wait_ge(up_mid, 8 * g + 2 * y)
                pair = y % 2
                scale_out(c_done, acc[:, 2 * pair:2 * pair + 2, :], up_pad[:, :, 1:S + 1])

            def up_taps(g, y):
                for k in (0, 2):
                    for t in range(2):
                        f = FT * (y // 2) + 2 * (y % 2) + t
                        if k == 0:
                            dve.wait_ge(up_mid, 8 * g + (2 * y + t + 1))
                        else:
                            dve.wait_ge(up_side, 16 * g + (4 * y + t + 1))
                        v.scalar_tensor_tensor(out=up_conv[:, t, :], in0=up_pad[:, t, k:k + S],
                                               scalar=param(3 * KC * g + (C_FW + 3 * f + k)), in1=up_conv[:, t, :],
                                               op0=ALU.mult, op1=ALU.add).then_inc(up_side, 1)

            def hidden(g, y):
                dve.wait_ge(up_side, 16 * g + (4 * y + 12))
                dve.wait_ge(gate_act, 2 * g + (y + 1))
                v.tensor_tensor(gated[:, 2 * y:2 * y + 2, :], gated[:, 2 * y:2 * y + 2, :], up_conv[:], ALU.mult
                                ).then_inc(hidden_ready, 1)

            def hidden_low(g, y):
                dve.wait_ge(hid_high_ready, 2 * g + (y + 1))
                high, low = (last_high, last_low) if is_last(g) else (hid_high, hid_low)
                v.tensor_tensor(low[:, 2 * y:2 * y + 2, :], gated[:, 2 * y:2 * y + 2, :],
                                high[:, 2 * y:2 * y + 2, :].bitcast(F32), ALU.subtract).then_inc(hid_low_ready, 1)

            def ffn_slot(g, s, c):
                first = isinstance(g, int)
                if s == 0 and needs_wait(g):
                    up_out(g - 1, 3, c)
                if s == 4:
                    if not needs_wait(g):
                        dve.wait_ge(turn_read, t_use("F", "ROW"))
                    up_out(g, 0, c)
                if s == (16 if first else 8):
                    up_out(g, 1, c)
                if 9 <= s <= 16 and not first:
                    res_add(s - 9, g, c)
                if s == 20:
                    up_out(g, 2, c)
                split_low(c + 1, c + 1 if first else s + 1)
                if s == 0 and needs_wait(g):
                    up_taps(g - 1, 3)
                if s == 1 and needs_wait(g):
                    hidden(g - 1, 1)
                if s == 3 and needs_wait(g):
                    hidden_low(g - 1, 1)
                if s == 4:
                    up_taps(g, 0)
                if s == (16 if first else 8):
                    up_taps(g, 1)
                if s == 20:
                    up_taps(g, 2)
                if s == 21:
                    hidden(g, 0)
                if s == 23:
                    hidden_low(g, 0)

            res_add(7, GC + 7, F0)
            for n in range(2):
                v.memset(up_pad[:, :, n * (S + 1):n * (S + 1) + 1], 0.0).then_inc(ffn_pads, 1)
            dve.wait_ge(ffn_pads, 2)
            for l, s in enumerate(FIRST_SLOTS):
                ffn_slot(0, s, F0 + l)
                if l == 0:
                    h2_low_pair(7)
                if l == 2:
                    invert("COL", 2 * PAIRS + 3, rms_col, 4)
            with dve.Fori(1, GROUPS - 1) as g:
                for s in range(F_SLOTS):
                    ffn_slot(g, s, F_SLOTS * g + (F1 - F_SLOTS + s))
            for l, s in enumerate(FIRST_SLOTS):
                ffn_slot(GROUPS - 1, s, LAST + l)
            for l in range(17):
                if l == 0:
                    up_out(GROUPS - 1, 3, LAST + 16)
                elif l < 16:
                    res_add((l - 1) % 8, l - 1, LAST + 16 + l)
                else:
                    for t in range(2):
                        dve.wait_ge(chunk_done, SLOTS + t)
                        v.tensor_tensor(res[:, DT - 2 + t, :], res[:, DT - 2 + t, :], acc[:, 2 + t, :], ALU.add
                                        ).then_inc(emptied, 1)
                if l < 15:
                    split_low(LAST + l + 17, l + 17)
                if l == 0:
                    up_taps(GROUPS - 1, 3)
                if l == 1:
                    hidden(GROUPS - 1, 1)
                if l == 3:
                    hidden_low(GROUPS - 1, 1)

        @block.tensor
        def _(pe):
            mm = nc.tensor.matmul

            def multiply(c, s, dst, high, low, first, last, ready=None, middle=None):
                if needs_wait(c):
                    pe.wait_ge(w_low_ready, c + 1)
                for j in range(KC):
                    if ready is not None:
                        ready(j)
                    if middle is not None and j == KC // 2:
                        middle()
                    for t in range(2):
                        at = NC * j + P * t
                        wh, wl = w_high[:, s % 2, at:at + P], w_low[:, s % 2, at:at + P]
                        mm(dst[:, t, :], wh, high(j), start=first and j == 0, stop=False)
                        mm(dst[:, t, :], wh, low(j), start=False, stop=False)
                        done = mm(dst[:, t, :], wl, high(j), start=False, stop=last and j == KC - 1)
                done.then_inc(chunk_done, 1)

            def h_tiles(tile0):
                return (lambda j: h_high[:, tile0 + j, :]), (lambda j: h_low[:, tile0 + j, :])

            def next_turn(i, name):
                if not (i == 0 and name == "XCOL" if isinstance(i, int) else False):
                    pe.wait_ge(turn_read, t_use(i, name) - 1)

            def token_sums(col):
                for t in range(QT):
                    last = mm(turn[:, t:t + 1], square_sum[:, 0, P * t:P * (t + 1)], const_col(col), start=True,
                              stop=True)
                last.then_inc(turn_made, 1)

            def head_sums():
                for hh in range(2):
                    for t in range(QT):
                        last = mm(turn[:, QT * hh + t:QT * hh + t + 1], squares[:, hh, P * t:P * (t + 1)],
                                  const_col(K_MEAN_H), start=True, stop=True)
                last.then_inc(turn_made, 1)

            def spread_cols(bank, cols):
                for t in range(QT):
                    last = mm(bank[:, P * t:P * (t + 1)], cols[:, t:t + 1].broadcast_to([P, P]), ident,
                              start=True, stop=True)
                return last

            def attention_slot(i, j, s):
                if s == 1:
                    pe.wait_ge(qk_low_ready, 2 * j + 2)
                    pe.wait_ge(emptied, 5 * j + 5)
                if s in (1, 2):
                    next_turn(i, f"V{s - 1}")
                    for t in range(QT):
                        last = nc.tensor.transpose(turn[:, P * t:P * (t + 1)],
                                                   mixed[:, DT - 3 + s, P * t:P * (t + 1)], ident)
                    last.then_inc(turn_made, 1)
                if s in (5, 7, 9, 11):
                    u = s - 4
                    pe.wait_ge(turn_read, t_use(i, f"P{u}"))
                    if u == 5:
                        pe.wait_ge(o_read, 2 * j + 1)
                    hh, q0 = u // 4, P * (u % 4 - 1)
                    for t in range(QT):
                        vh, vl = v_high[:, hh, P * t:P * (t + 1)], v_low[:, hh, P * t:P * (t + 1)]
                        out_t = attn_o[:, q0:q0 + 2 * P]
                        mm(out_t, vh, probs_t_high[:, t, :], start=t == 0, stop=False)
                        mm(out_t, vh, probs_t_low[:, t, :], start=False, stop=False)
                        last = mm(out_t, vl, probs_t_high[:, t, :], start=False, stop=t == QT - 1)
                    last.then_inc(pv_done, 1)
                if 3 <= s <= 10:
                    u = s - 3
                    next_turn(i, f"P{u}")
                    pe.wait_ge(probs_ready, 8 * j + (u + 1))
                    for t in range(QT):
                        last = nc.tensor.transpose(turn[:, P * t:P * (t + 1)], probs[:, u % 2, P * t:P * (t + 1)], ident)
                    last.then_inc(turn_made, 1)
                if 1 <= s <= 8:
                    u = s - 1
                    if u >= 2:
                        pe.wait_ge(score_read, 8 * j + (u - 1))
                    hh, q0 = u // 4, P * (u % 4)
                    qh, ql = q_high[:, hh, q0:q0 + P], q_low[:, hh, q0:q0 + P]
                    mm(score[:, u % 2, :], qh, k_high[:, hh, :], start=True, stop=False)
                    mm(score[:, u % 2, :], qh, k_low[:, hh, :], start=False, stop=False)
                    mm(score[:, u % 2, :], ql, k_high[:, hh, :], start=False, stop=True).then_inc(score_made, 1)

            def x_mean_square():
                pe.wait_ge(squares_added, DT // 2 + 1)
                token_sums(K_MEAN_D)

            def x_row():
                pe.wait_ge(inverse_ready, 1)
                spread_cols(turn, rms_col).then_inc(turn_made, 1)

            def iteration(i):
                first = isinstance(i, int)
                c0 = I_SLOTS * i
                for s in range(I_SLOTS):
                    if first and s == 4:
                        pe.wait_ge(const_in, 16)
                    if not first:
                        attention_slot(i, i - 1, s)
                    if s == 14:
                        next_turn(i, "Q")
                        pe.wait_ge(head_squares, 2 * i + 1)
                        head_sums()
                    if s == 17:
                        next_turn(i, "K")
                        pe.wait_ge(head_squares, 2 * i + 2)
                        head_sums()
                    if s == 19:
                        pe.wait_ge(inverse_ready, 2 * i + 3)
                        if not first:
                            pe.wait_ge(o_read, 2 * i)
                        spread_cols(turn, rk_col[:, 0:QT])
                        spread_cols(attn_o, rk_col[:, QT:2 * QT]).then_inc(k_spread, 1)
                    y = s // 4
                    if s % 4 == 0 and y in (2, 3):
                        pe.wait_ge(emptied, 5 * i + (y - 1))
                    if s % 4 == 0 and y in (0, 1) and not first:
                        pe.wait_ge(emptied, 5 * i + (y - 2))
                    if s % 4 == 0 and y == 4 and not first:
                        pe.wait_ge(score_read, 8 * i)
                    dst = score if y == 4 else acc[:, 2 * (y % 2):2 * (y % 2) + 2, :]
                    tile0 = KC * (s % 4)
                    ready = None
                    if first and s < 4:
                        def ready(j, tile0=tile0):
                            pe.wait_ge(x_low_ready, tile0 + j + 1)
                            if tile0 == 0 and j < KC - 1:
                                pe.wait_ge(w0_low, j + 1)
                            elif tile0 == 0:
                                pe.wait_ge(w_low_ready, 1)
                    middle = {6: x_mean_square, 7: x_row}.get(s) if first else None
                    multiply(c0 + s, s, dst, *h_tiles(tile0), s % 4 == 0, s % 4 == 3, ready, middle)

            iteration(0)
            with pe.Fori(1, PAIRS) as i:
                iteration(i)

            def layer_norm_mean():
                next_turn("A", "MU")
                pe.wait_ge(conv_added, CT)
                mm(turn[:], const_col(K_MEAN_C).broadcast_to([P, P]), conv_sum, start=True, stop=True
                   ).then_inc(turn_made, 1)

            def layer_norm_variance():
                next_turn("A", "VAR")
                pe.wait_ge(centred_added, CT // 2)
                token_sums(K_MEAN_C)

            def layer_norm_row():
                next_turn("A", "ROW")
                pe.wait_ge(inverse_ready, 2 * PAIRS + 2)
                spread_cols(turn, rms_col).then_inc(turn_made, 1)

            def acc_of(group):
                pe.wait_ge(emptied, group - 1)
                return acc[:, 2 * (group % 2):2 * (group % 2) + 2, :]

            def early_ready(j):
                if j % 2 == 0:
                    pe.wait_ge(mix_low_ready, 1 + j // 2)

            for s in range(8):
                if s == 6:
                    layer_norm_row()
                multiply(A0 + s, s, acc_of(GA + s), lambda j: early_high[:, j, :], lambda j: early_low[:, j, :],
                         True, True, early_ready if s == 0 else None,
                         {2: layer_norm_mean, 5: layer_norm_variance}.get(s))

            for s in range(16):
                attention_slot("B", PAIRS - 1, s)
                ready = None
                if s < 2:
                    def ready(j, tile0=KC * s):
                        if j % 2 == 0:
                            pe.wait_ge(mix_low_ready, 3 + (tile0 + j) // 2)
                multiply(B0 + s, s, acc_of(GB + s // 2), *h_tiles(KC * (s % 2)), s % 2 == 0, s % 2 == 1, ready)

            pe.wait_ge(mix_low_ready, 8)
            for n in range(8):
                multiply(C0 + n, n, acc_of(GC + n), *h_tiles(3 * KC), True, True)

            def up_slot(g, s, c):
                if s % 4 == 0:
                    pe.wait_ge(emptied, up_group(g, s // 4) - 1)
                tile0, pair = KC * (s % 4), (s // 4) % 2
                ready = None
                if not needs_wait(g) and s < 4:
                    def ready(j, tile0=tile0):
                        pe.wait_ge(h2_low_ready, tile0 + j + 1)
                multiply(c, s, acc[:, 2 * pair:2 * pair + 2, :], lambda j: h2_high[:, tile0 + j, :],
                         lambda j: h2_low[:, tile0 + j, :], s % 4 == 0, s % 4 == 3, ready)

            def down_slot(g, n, c):
                if n == 0:
                    pe.wait_ge(hid_low_ready, 2 * g + 2)
                pe.wait_ge(emptied, down_group(g, n) - 1)
                high, low = (last_high, last_low) if is_last(g) else (hid_high, hid_low)
                multiply(c, n, acc[:, 2 * (n % 2):2 * (n % 2) + 2, :], lambda j: high[:, j, :],
                         lambda j: low[:, j, :], True, True)

            for s in range(16):
                if s == 2:
                    next_turn("F", "COL")
                    pe.wait_ge(res_squares_added, DT // 2 + 1)
                    token_sums(K_MEAN_D)
                if s == 3:
                    next_turn("F", "ROW")
                    pe.wait_ge(inverse_ready, 2 * PAIRS + 3)
                    spread_cols(turn, rms_col).then_inc(turn_made, 1)
                up_slot(0, s, F0 + s)
            with pe.Fori(1, GROUPS - 1) as g:
                c = F_SLOTS * g + (F1 - F_SLOTS)
                for s in range(8):
                    up_slot(g, s, c + s)
                for n in range(8):
                    down_slot(g - 1, n, c + (8 + n))
                for s in range(8, 16):
                    up_slot(g, s, c + (8 + s))
            for s in range(16):
                up_slot(GROUPS - 1, s, LAST + s)
            for n in range(8):
                down_slot(GROUPS - 2, n, LAST + 16 + n)
            for n in range(7):
                down_slot(GROUPS - 1, n, LAST + 24 + n)
            pe.wait_ge(emptied, down_group(GROUPS - 1, 7) - 1)
            pe.wait_ge(w_low_ready, SLOTS)
            for t in range(2):
                for j in range(KC):
                    at = NC * j + P * t
                    wh, wl = w_high[:, 1, at:at + P], w_low[:, 1, at:at + P]
                    mm(acc[:, 2 + t, :], wh, last_high[:, j, :], start=j == 0, stop=False)
                    mm(acc[:, 2 + t, :], wh, last_low[:, j, :], start=False, stop=False)
                    done = mm(acc[:, 2 + t, :], wl, last_high[:, j, :], start=False, stop=j == KC - 1)
                done.then_inc(chunk_done, 1)


def is_last(g):
    return isinstance(g, int) and g == GROUPS - 1


def needs_wait(i):
    return not (isinstance(i, int) and i == 0)


def constant_table():
    con = np.zeros((P, K_ALL), np.float32)
    con[:, K_ID:K_ID + P] = np.eye(P)
    offset = np.arange(BIAS_W)[None, :] - (S - P) - np.arange(P)[:, None]
    count = sum(((np.abs(offset) <= w // 2) & (offset % d == 0)).astype(int) for w, d in PATTERNS)
    con[:, K_DIST:K_DIST + BIAS_W] = np.abs(offset)
    con[:, K_LOGN:K_LOGN + BIAS_W] = np.where(count > 0, np.log(np.maximum(count, 1)), -1e30)
    con[:, K_MEAN_D] = 1 / D
    con[:, K_MEAN_C] = 1 / (CT * P)
    con[:, K_MEAN_H] = 1 / P
    con[:, K_EPS_R] = 1e-6
    con[:, K_EPS_L] = 1e-5
    con[:, K_SLOPE:K_SLOPE + HEADS] = [-2.0 ** (-8.0 * (h + 1) / HEADS) for h in range(HEADS)]
    return con


def channel_major(a):
    a = np.ascontiguousarray(a)
    a = a.reshape(1, -1) if a.ndim == 1 else a
    k, n = a.shape
    return a.reshape(k, n // P, P).transpose(2, 1, 0).reshape(P, -1)


def kernel(x, norm1_g, w_in, conv_dw_w, conv_dw_b, conv_ln_g, conv_ln_b, q_norm_g, k_norm_g, w_out, norm2_g,
           w_up, ffn_dw_w, ffn_dw_b, w_down):
    import concourse.bacc as bacc
    from concourse.bass_utils import run_bass_kernel_spmd

    params = np.concatenate([channel_major(a) for a in (
        norm1_g, norm2_g, conv_dw_w, conv_dw_b, conv_ln_g, conv_ln_b, q_norm_g, k_norm_g, ffn_dw_w, ffn_dw_b)], axis=1)
    arrays = {
        "x_t": np.ascontiguousarray(np.asarray(x)[0].T.reshape(DT, P, S).transpose(1, 0, 2)),
        "w_in": np.ascontiguousarray(w_in),
        "w_out": np.ascontiguousarray(w_out),
        "w_up": np.ascontiguousarray(w_up),
        "w_down": np.ascontiguousarray(w_down),
        "params": np.ascontiguousarray(params),
        "consts": constant_table(),
    }
    nc = bacc.Bacc("TRN2", target_bir_lowering=False, num_devices=1, dynamic_dma_scratch_size=1024)
    args = [nc.dram_tensor(f"{n}_dram", a.shape, F32, kind="ExternalInput").ap() for n, a in arrays.items()]
    out = nc.dram_tensor("out_dram", (P, DT, S), F32, kind="ExternalOutput").ap()
    hybrid_encoder_layer(nc, *args, out)
    result = run_bass_kernel_spmd(nc, [{f"{n}_dram": a for n, a in arrays.items()}], core_ids=[0])
    y = result.results[0]["out_dram"]
    return np.ascontiguousarray(y.transpose(1, 0, 2).reshape(D, S).T)[None]
```
